# Optimizing a Trainium2 kernel written in Bass

```python
import numpy as np
import jax
import jax.numpy as jnp
from jax import lax
import jax, jax.numpy as jnp

D_MODEL = 1024
BATCH = 1
SEQ = 256
DEPTH = 2

N_MIXERS = 3
HEAD_DIM = 64
N_HEADS = D_MODEL // HEAD_DIM
D_FF = 2816
RMS_EPS = 1e-6
ROPE_THETA = 10000.0
BLOCK_Q = 128
NEG = -1e30

NSA_GROUPS = 4
NSA_REP = N_HEADS // NSA_GROUPS
NSA_CMP_LEN = 32
NSA_CMP_STRIDE = 16
NSA_CMP_HIDDEN = 2 * HEAD_DIM
NSA_SLC_LEN = 64
NSA_TOPK = 16
NSA_WINDOW = 512
NSA_SLC_QBLOCK = 32
NSA_FORCE_BONUS = 1e4

SWA_KV_HEADS = 2
SWA_REP = N_HEADS // SWA_KV_HEADS
SWA_WINDOW = 128

FOX_HEADS = N_HEADS

N_A = len(range(0, DEPTH, N_MIXERS))
N_B = len(range(1, DEPTH, N_MIXERS))
N_C = len(range(2, DEPTH, N_MIXERS))

Q_WIDTH = N_HEADS * HEAD_DIM
NSA_KV_WIDTH = 3 * 2 * NSA_GROUPS * HEAD_DIM
NSA_IN = Q_WIDTH + NSA_KV_WIDTH + 3 * N_HEADS
SWA_IN = Q_WIDTH + 2 * SWA_KV_HEADS * HEAD_DIM
FOX_IN = 3 * FOX_HEADS * HEAD_DIM + FOX_HEADS


def rmsnorm(x, g):
    xf = x.astype(jnp.float32)
    y = xf * lax.rsqrt(jnp.mean(xf * xf, axis=-1, keepdims=True) + RMS_EPS)
    return (y * g.astype(jnp.float32)).astype(x.dtype)

def swiglu(x, w_gu, w_down):
    g, u = jnp.split(x @ w_gu, 2, axis=-1)
    return (jax.nn.silu(g) * u) @ w_down

def rope_tables(S):
    inv = ROPE_THETA ** (-jnp.arange(0, HEAD_DIM, 2, dtype=jnp.float32) / HEAD_DIM)
    ang = jnp.arange(S, dtype=jnp.float32)[:, None] * inv[None, :]
    return jnp.cos(ang), jnp.sin(ang)

def apply_rope(x, cos, sin):
    x1, x2 = jnp.split(x.astype(jnp.float32), 2, axis=-1)
    c = cos[None, :, None, :]
    s = sin[None, :, None, :]
    return jnp.concatenate([x1 * c - x2 * s, x2 * c + x1 * s], axis=-1).astype(x.dtype)

def banded_attention(q, k, v, window, sinks=None):
    B, S, G, R, dh = q.shape
    span = window + BLOCK_Q
    kp = jnp.pad(k, ((0, 0), (window, 0), (0, 0), (0, 0)))
    vp = jnp.pad(v, ((0, 0), (window, 0), (0, 0), (0, 0)))
    scale = dh ** -0.5

    def step(i):
        start = i * BLOCK_Q
        qi = lax.dynamic_slice_in_dim(q, start, BLOCK_Q, axis=1)
        ki = lax.dynamic_slice_in_dim(kp, start, span, axis=1)
        vi = lax.dynamic_slice_in_dim(vp, start, span, axis=1)
        s = jnp.einsum('bqgrd,bkgd->bgrqk', qi, ki).astype(jnp.float32) * scale
        qpos = start + jnp.arange(BLOCK_Q)
        kpos = start - window + jnp.arange(span)
        diff = qpos[:, None] - kpos[None, :]
        mask = (diff >= 0) & (diff < window) & (kpos[None, :] >= 0)
        s = jnp.where(mask, s, NEG)
        if sinks is None:
            p = jax.nn.softmax(s, axis=-1)
        else:
            sk = sinks.astype(jnp.float32)[None, :, :, None, None]
            m = jnp.maximum(jnp.max(s, axis=-1, keepdims=True), sk)
            e = jnp.exp(s - m)
            p = e / (jnp.sum(e, axis=-1, keepdims=True) + jnp.exp(sk - m))
        return jnp.einsum('bgrqk,bkgd->bqgrd', p.astype(vi.dtype), vi)

    o = lax.map(step, jnp.arange(S // BLOCK_Q))
    return jnp.moveaxis(o, 0, 1).reshape(B, S, G, R, dh)

def compress_blocks(x, blk_idx, pe, w1, w2):
    B, _, G, dh = x.shape
    n_cmp, L = blk_idx.shape
    xb = x[:, blk_idx] + pe[:, None, :]
    xb = xb.transpose(0, 1, 3, 2, 4).reshape(B, n_cmp, G, L * dh)
    return jax.nn.gelu(xb @ w1) @ w2

def cmp_to_slc_overlap(n_cmp, n_slc):
    cs = np.arange(n_cmp) * NSA_CMP_STRIDE
    ce = cs + NSA_CMP_LEN
    ss = np.arange(n_slc) * NSA_SLC_LEN
    se = ss + NSA_SLC_LEN
    ov = np.clip(np.minimum(ce[:, None], se[None, :]) - np.maximum(cs[:, None], ss[None, :]), 0, None)
    return jnp.asarray(ov / NSA_CMP_LEN, dtype=jnp.float32)

def selected_block_attention(q, k, v, sel):
    B, S, G, R, dh = q.shape
    n_sel = sel.shape[-1]
    n_slc = S // NSA_SLC_LEN
    m = n_sel * NSA_SLC_LEN
    kblk = k.reshape(B, n_slc, NSA_SLC_LEN, G, dh).transpose(0, 3, 1, 2, 4)
    vblk = v.reshape(B, n_slc, NSA_SLC_LEN, G, dh).transpose(0, 3, 1, 2, 4)
    gather = jax.vmap(jax.vmap(lambda blocks, ids: blocks[ids]))
    offs = jnp.arange(NSA_SLC_LEN)
    scale = dh ** -0.5

    def step(i):
        start = i * NSA_SLC_QBLOCK
        qi = lax.dynamic_slice_in_dim(q, start, NSA_SLC_QBLOCK, axis=1)
        ids = lax.dynamic_slice_in_dim(sel, start, NSA_SLC_QBLOCK, axis=2)
        kg = gather(kblk, ids).reshape(B, G, NSA_SLC_QBLOCK, m, dh)
        vg = gather(vblk, ids).reshape(B, G, NSA_SLC_QBLOCK, m, dh)
        kpos = (ids[..., None] * NSA_SLC_LEN + offs).reshape(B, G, NSA_SLC_QBLOCK, m)
        qpos = start + jnp.arange(NSA_SLC_QBLOCK)
        mask = (kpos <= qpos[:, None])[:, :, None]
        s = jnp.einsum('bqgrd,bgqmd->bgrqm', qi, kg).astype(jnp.float32) * scale
        p = jax.nn.softmax(jnp.where(mask, s, NEG), axis=-1)
        return jnp.einsum('bgrqm,bgqmd->bqgrd', p.astype(vg.dtype), vg)

    o = lax.map(step, jnp.arange(S // NSA_SLC_QBLOCK))
    return jnp.moveaxis(o, 0, 1).reshape(B, S, G, R, dh)

def nsa_mixer(h, cos, sin, w_in, ck_pe, ck_w1, ck_w2, cv_pe, cv_w1, cv_w2, w_out):
    B, S, _ = h.shape
    G, R, dh = NSA_GROUPS, NSA_REP, HEAD_DIM
    scale = dh ** -0.5
    proj = h @ w_in
    q = apply_rope(proj[..., :Q_WIDTH].reshape(B, S, N_HEADS, dh), cos, sin).reshape(B, S, G, R, dh)
    kv = proj[..., Q_WIDTH:Q_WIDTH + NSA_KV_WIDTH].reshape(B, S, 3, 2, G, dh)
    gates = jax.nn.sigmoid(proj[..., Q_WIDTH + NSA_KV_WIDTH:].astype(jnp.float32)).reshape(B, S, 3, G, R, 1)
    k = apply_rope(kv[:, :, :, 0].reshape(B, S, 3 * G, dh), cos, sin).reshape(B, S, 3, G, dh)
    v = kv[:, :, :, 1]
    t = jnp.arange(S)

    n_cmp = (S - NSA_CMP_LEN) // NSA_CMP_STRIDE + 1
    blk_idx = jnp.arange(n_cmp)[:, None] * NSA_CMP_STRIDE + jnp.arange(NSA_CMP_LEN)[None, :]
    k_cmp = compress_blocks(k[:, :, 0], blk_idx, ck_pe, ck_w1, ck_w2)
    v_cmp = compress_blocks(v[:, :, 0], blk_idx, cv_pe, cv_w1, cv_w2)
    s_cmp = jnp.einsum('bsgrd,bngd->bgrsn', q, k_cmp).astype(jnp.float32) * scale
    cmp_valid = (jnp.arange(n_cmp) * NSA_CMP_STRIDE + NSA_CMP_LEN - 1)[None, :] <= t[:, None]
    p_cmp = jax.nn.softmax(jnp.where(cmp_valid, s_cmp, NEG), axis=-1) * cmp_valid
    o_cmp = jnp.einsum('bgrsn,bngd->bsgrd', p_cmp.astype(v_cmp.dtype), v_cmp)

    n_slc = S // NSA_SLC_LEN
    k_sel = min(NSA_TOPK, n_slc)
    imp = jnp.einsum('bgrsn,nj->bgsj', p_cmp, cmp_to_slc_overlap(n_cmp, n_slc))
    tb = (t // NSA_SLC_LEN)[:, None]
    j = jnp.arange(n_slc)[None, :]
    forced = (j == 0) | (j == tb) | (j == tb - 1)
    imp = jnp.where(j > tb, NEG, jnp.where(forced, NSA_FORCE_BONUS, imp))
    _, sel = lax.top_k(imp, k_sel)
    o_slc = selected_block_attention(q, k[:, :, 1], v[:, :, 1], sel)

    o_win = banded_attention(q, k[:, :, 2], v[:, :, 2], NSA_WINDOW)

    o = gates[:, :, 0] * o_cmp + gates[:, :, 1] * o_slc + gates[:, :, 2] * o_win
    return o.astype(h.dtype).reshape(B, S, Q_WIDTH) @ w_out

def swa_mixer(h, cos, sin, w_in, sinks, w_out):
    B, S, _ = h.shape
    proj = h @ w_in
    q = apply_rope(proj[..., :Q_WIDTH].reshape(B, S, N_HEADS, HEAD_DIM), cos, sin)
    q = q.reshape(B, S, SWA_KV_HEADS, SWA_REP, HEAD_DIM)
    kv = proj[..., Q_WIDTH:].reshape(B, S, 2, SWA_KV_HEADS, HEAD_DIM)
    k = apply_rope(kv[:, :, 0], cos, sin)
    v = kv[:, :, 1]
    o = banded_attention(q, k, v, SWA_WINDOW, sinks.reshape(SWA_KV_HEADS, SWA_REP))
    return o.reshape(B, S, Q_WIDTH) @ w_out

def fox_mixer(h, w_in, b_f, w_out):
    B, S, _ = h.shape
    dh = HEAD_DIM
    scale = dh ** -0.5
    proj = h @ w_in
    qkv = proj[..., :3 * FOX_HEADS * dh].reshape(B, S, 3, FOX_HEADS, dh)
    q, k, v = qkv[:, :, 0], qkv[:, :, 1], qkv[:, :, 2]
    log_f = jax.nn.log_sigmoid((proj[..., 3 * FOX_HEADS * dh:] + b_f).astype(jnp.float32))
    c = jnp.cumsum(log_f, axis=1).transpose(0, 2, 1)
    kpos = jnp.arange(S)

    def step(i):
        start = i * BLOCK_Q
        qi = lax.dynamic_slice_in_dim(q, start, BLOCK_Q, axis=1)
        ci = lax.dynamic_slice_in_dim(c, start, BLOCK_Q, axis=2)
        s = jnp.einsum('bqhd,bkhd->bhqk', qi, k).astype(jnp.float32) * scale
        s = s + ci[..., None] - c[:, :, None, :]
        qpos = start + jnp.arange(BLOCK_Q)
        p = jax.nn.softmax(jnp.where(kpos[None, :] <= qpos[:, None], s, NEG), axis=-1)
        return jnp.einsum('bhqk,bkhd->bqhd', p.astype(v.dtype), v)

    o = lax.map(step, jnp.arange(S // BLOCK_Q))
    return jnp.moveaxis(o, 0, 1).reshape(B, S, FOX_HEADS * dh) @ w_out

def first_inputs(seed: int = 0) -> dict:
    key = jax.random.key(seed)
    ks = iter(jax.random.split(key, 32))
    f32 = jnp.float32

    def nrm(shape, scale):
        return scale * jax.random.normal(next(ks), shape, f32)

    def gain(shape):
        return 1.0 + 0.01 * jax.random.normal(next(ks), shape, f32)

    L, dh, Hc = NSA_CMP_LEN, HEAD_DIM, NSA_CMP_HIDDEN
    return {
        'x': nrm((BATCH, SEQ, D_MODEL), 1.0),
        'ffn1_norm': gain((DEPTH, D_MODEL)),
        'ffn1_w_gu': nrm((DEPTH, D_MODEL, 2 * D_FF), D_MODEL ** -0.5),
        'ffn1_w_down': nrm((DEPTH, D_FF, D_MODEL), D_FF ** -0.5),
        'mix_norm': gain((DEPTH, D_MODEL)),
        'ffn2_norm': gain((DEPTH, D_MODEL)),
        'ffn2_w_gu': nrm((DEPTH, D_MODEL, 2 * D_FF), D_MODEL ** -0.5),
        'ffn2_w_down': nrm((DEPTH, D_FF, D_MODEL), D_FF ** -0.5),
        'nsa_w_in': nrm((N_A, D_MODEL, NSA_IN), D_MODEL ** -0.5),
        'nsa_ck_pe': nrm((N_A, L, dh), 0.1),
        'nsa_ck_w1': nrm((N_A, L * dh, Hc), (L * dh) ** -0.5),
        'nsa_ck_w2': nrm((N_A, Hc, dh), Hc ** -0.5),
        'nsa_cv_pe': nrm((N_A, L, dh), 0.1),
        'nsa_cv_w1': nrm((N_A, L * dh, Hc), (L * dh) ** -0.5),
        'nsa_cv_w2': nrm((N_A, Hc, dh), Hc ** -0.5),
        'nsa_w_out': nrm((N_A, Q_WIDTH, D_MODEL), Q_WIDTH ** -0.5),
        'swa_w_in': nrm((N_B, D_MODEL, SWA_IN), D_MODEL ** -0.5),
        'swa_sinks': nrm((N_B, N_HEADS), 1.0),
        'swa_w_out': nrm((N_B, Q_WIDTH, D_MODEL), Q_WIDTH ** -0.5),
        'fox_w_in': nrm((N_C, D_MODEL, FOX_IN), D_MODEL ** -0.5),
        'fox_b_f': jax.random.uniform(next(ks), (N_C, FOX_HEADS), f32, 1.0, 4.0),
        'fox_w_out': nrm((N_C, FOX_HEADS * HEAD_DIM, D_MODEL), (FOX_HEADS * HEAD_DIM) ** -0.5),
        'final_norm': gain((D_MODEL,)),
    }

def first_block(x, ffn1_norm, ffn1_w_gu, ffn1_w_down, mix_norm, ffn2_norm, ffn2_w_gu, ffn2_w_down,
              nsa_w_in, nsa_ck_pe, nsa_ck_w1, nsa_ck_w2, nsa_cv_pe, nsa_cv_w1, nsa_cv_w2, nsa_w_out,
              swa_w_in, swa_sinks, swa_w_out, fox_w_in, fox_b_f, fox_w_out, final_norm):
    S = x.shape[1]
    cos, sin = rope_tables(S)
    for i in range(DEPTH):
        kind, j = i % N_MIXERS, i // N_MIXERS
        x = x + 0.5 * swiglu(rmsnorm(x, ffn1_norm[i]), ffn1_w_gu[i], ffn1_w_down[i])
        h = rmsnorm(x, mix_norm[i])
        if kind == 0:
            y = nsa_mixer(h, cos, sin, nsa_w_in[j], nsa_ck_pe[j], nsa_ck_w1[j], nsa_ck_w2[j],
                          nsa_cv_pe[j], nsa_cv_w1[j], nsa_cv_w2[j], nsa_w_out[j])
        elif kind == 1:
            y = swa_mixer(h, cos, sin, swa_w_in[j], swa_sinks[j], swa_w_out[j])
        else:
            y = fox_mixer(h, fox_w_in[j], fox_b_f[j], fox_w_out[j])
        x = x + y
        x = x + 0.5 * swiglu(rmsnorm(x, ffn2_norm[i]), ffn2_w_gu[i], ffn2_w_down[i])
    return rmsnorm(x, final_norm)


DEPTH_2 = 1

ATTN_HEADS = 8
ATTN_WIDTH = D_MODEL // 2
ATTN_HEAD_DIM = ATTN_WIDTH // ATTN_HEADS
MLSTM_HEADS = 4
MLSTM_WIDTH = D_MODEL - ATTN_WIDTH
MLSTM_HEAD_DIM = MLSTM_WIDTH // MLSTM_HEADS
IN_COLS = 3 * ATTN_WIDTH + 2 * MLSTM_WIDTH
CONV_WIDTH = 4
MLSTM_CHUNK = 64
MOBA_BLOCK = 256
MOBA_TOPK = 3
MOBA_QCHUNK = 32
D_FF_2 = ((8 * D_MODEL // 3 + 127) // 128) * 128
N_MOD = 9
EPS = 1e-6


def rmsnorm_2(x, g):
    xf = x.astype(jnp.float32)
    y = xf * lax.rsqrt(jnp.mean(xf * xf, axis=-1, keepdims=True) + EPS)
    return (y * g.astype(jnp.float32)).astype(x.dtype)

def modulate(h, shift, scale):
    return h * (1 + scale) + shift

def swiglu_2(h, w_gate, w_up, w_down):
    return (jax.nn.silu(h @ w_gate) * (h @ w_up)) @ w_down

def causal_depthwise_conv(x, w, b):
    C = x.shape[-1]
    out = lax.conv_general_dilated(x, w[:, None, :], window_strides=(1,),
                                   padding=((CONV_WIDTH - 1, 0),),
                                   dimension_numbers=('NWC', 'WIO', 'NWC'),
                                   feature_group_count=C)
    return out + b

def moba_attention(q, k, v):
    B, H, S, d = q.shape
    s_pad = -(-S // MOBA_BLOCK) * MOBA_BLOCK
    pad = s_pad - S
    if pad:
        padw = ((0, 0), (0, 0), (0, pad), (0, 0))
        q, k, v = jnp.pad(q, padw), jnp.pad(k, padw), jnp.pad(v, padw)
    nb = s_pad // MOBA_BLOCK
    topk = min(MOBA_TOPK, nb)
    k_blocks = k.reshape(B, H, nb, MOBA_BLOCK, d)
    v_blocks = v.reshape(B, H, nb, MOBA_BLOCK, d)
    k_mean = jnp.mean(k_blocks.astype(jnp.float32), axis=3)
    gate = jnp.einsum('bhsd,bhnd->bhsn', q.astype(jnp.float32), k_mean)
    q_block = jnp.arange(s_pad) // MOBA_BLOCK
    fully_past = jnp.arange(nb)[None, :] < q_block[:, None]
    gate = jnp.where(fully_past, gate, -jnp.inf)
    top_val, top_idx = lax.top_k(gate, topk)
    sel_valid = jnp.isfinite(top_val)

    n_chunks = s_pad // MOBA_QCHUNK

    def to_chunks(a):
        return jnp.moveaxis(a.reshape(B, H, n_chunks, MOBA_QCHUNK, *a.shape[3:]), 2, 0)

    b_idx = jnp.arange(B)[:, None, None]
    h_idx = jnp.arange(H)[None, :, None]
    scale = d ** -0.5
    n_sel = topk * MOBA_BLOCK

    def attend_chunk(args):
        q_c, idx_c, valid_c, ci = args
        blk = ci * MOBA_QCHUNK // MOBA_BLOCK
        flat = idx_c.reshape(B, H, MOBA_QCHUNK * topk)
        k_sel = k_blocks[b_idx, h_idx, flat].reshape(B, H, MOBA_QCHUNK, n_sel, d)
        v_sel = v_blocks[b_idx, h_idx, flat].reshape(B, H, MOBA_QCHUNK, n_sel, d)
        s_sel = jnp.einsum('bhqd,bhqnd->bhqn', q_c, k_sel).astype(jnp.float32) * scale
        s_sel = jnp.where(jnp.repeat(valid_c, MOBA_BLOCK, axis=-1), s_sel, -jnp.inf)
        k_own = lax.dynamic_index_in_dim(k_blocks, blk, axis=2, keepdims=False)
        v_own = lax.dynamic_index_in_dim(v_blocks, blk, axis=2, keepdims=False)
        s_own = jnp.einsum('bhqd,bhkd->bhqk', q_c, k_own).astype(jnp.float32) * scale
        q_pos = ci * MOBA_QCHUNK + jnp.arange(MOBA_QCHUNK)
        k_pos = blk * MOBA_BLOCK + jnp.arange(MOBA_BLOCK)
        s_own = jnp.where(k_pos[None, :] <= q_pos[:, None], s_own, -jnp.inf)
        p = jax.nn.softmax(jnp.concatenate([s_sel, s_own], axis=-1), axis=-1).astype(v.dtype)
        return (jnp.einsum('bhqn,bhqnd->bhqd', p[..., :n_sel], v_sel)
                + jnp.einsum('bhqk,bhkd->bhqd', p[..., n_sel:], v_own))

    out = lax.map(attend_chunk, (to_chunks(q), to_chunks(top_idx), to_chunks(sel_valid),
                                 jnp.arange(n_chunks)))
    out = jnp.moveaxis(out, 0, 2).reshape(B, H, s_pad, d)
    return out[:, :, :S]

def mlstm_chunkwise(q, k, v, i_pre, log_f):
    B, H, S, d = q.shape
    L = MLSTM_CHUNK
    nc = S // L

    def chunks(a):
        return jnp.moveaxis(a.reshape(B, H, nc, L, *a.shape[3:]), 2, 0)

    qc, kc, vc, ic = chunks(q), chunks(k), chunks(v), chunks(i_pre)
    bc = jnp.cumsum(chunks(log_f), axis=-1)
    causal = jnp.tril(jnp.ones((L, L), dtype=bool))

    def step(carry, xs):
        C, n, m = carry
        q_, k_, v_, i_, b_ = xs
        log_d = jnp.where(causal, b_[..., :, None] - b_[..., None, :] + i_[..., None, :], -jnp.inf)
        log_inter = b_ + m[..., None]
        m_t = jnp.maximum(log_inter, jnp.max(log_d, axis=-1))
        w_intra = jnp.exp(log_d - m_t[..., None])
        w_inter = jnp.exp(log_inter - m_t)
        s = jnp.einsum('bhtd,bhsd->bhts', q_, k_) * w_intra
        num = (jnp.einsum('bhts,bhsv->bhtv', s, v_)
               + w_inter[..., None] * jnp.einsum('bhvk,bhtk->bhtv', C, q_))
        den = jnp.sum(s, axis=-1) + w_inter * jnp.einsum('bhk,bhtk->bht', n, q_)
        h = num / jnp.maximum(jnp.abs(den), jnp.exp(-m_t))[..., None]
        b_last = b_[..., -1]
        log_g = b_last[..., None] - b_ + i_
        m_new = jnp.maximum(b_last + m, jnp.max(log_g, axis=-1))
        w_g = jnp.exp(log_g - m_new[..., None])
        decay = jnp.exp(b_last + m - m_new)
        C = decay[..., None, None] * C + jnp.einsum('bhsv,bhsk->bhvk', v_ * w_g[..., None], k_)
        n = decay[..., None] * n + jnp.einsum('bhs,bhsk->bhk', w_g, k_)
        return (C, n, m_new), h

    init = (jnp.zeros((B, H, d, d), jnp.float32), jnp.zeros((B, H, d), jnp.float32),
            jnp.zeros((B, H), jnp.float32))
    _, h = lax.scan(step, init, (qc, kc, vc, ic, bc))
    return jnp.moveaxis(h, 0, 2).reshape(B, H, S, d)

def hybrid_mixer(h, w_in, conv_w, conv_b, w_q_m, w_k_m, w_v_m, w_if, b_if,
                 mlstm_norm, mlstm_skip, attn_norm, w_out):
    B, S, _ = h.shape
    proj = h @ w_in
    q_a, k_a, v_a, x_m, z = jnp.split(
        proj, [ATTN_WIDTH, 2 * ATTN_WIDTH, 3 * ATTN_WIDTH, 3 * ATTN_WIDTH + MLSTM_WIDTH], axis=-1)

    def heads_a(t):
        return t.reshape(B, S, ATTN_HEADS, ATTN_HEAD_DIM).transpose(0, 2, 1, 3)
    o_a = moba_attention(heads_a(q_a), heads_a(k_a), heads_a(v_a))
    o_a = rmsnorm_2(o_a.transpose(0, 2, 1, 3).reshape(B, S, ATTN_WIDTH), attn_norm)

    x_conv = jax.nn.silu(causal_depthwise_conv(x_m, conv_w, conv_b))
    def headwise(t, w):
        return jnp.einsum('bshd,hde->bshe', t.reshape(B, S, MLSTM_HEADS, MLSTM_HEAD_DIM), w)
    q_m = headwise(x_conv, w_q_m)
    k_m = headwise(x_conv, w_k_m)
    v_m = headwise(x_m, w_v_m)
    gates = (jnp.concatenate([q_m, k_m, v_m], axis=-1).reshape(B, S, 3 * MLSTM_WIDTH) @ w_if
             + b_if).astype(jnp.float32)
    i_pre = gates[..., :MLSTM_HEADS].transpose(0, 2, 1)
    log_f = jax.nn.log_sigmoid(gates[..., MLSTM_HEADS:]).transpose(0, 2, 1)
    to_h = lambda t: t.transpose(0, 2, 1, 3).astype(jnp.float32)
    h_m = mlstm_chunkwise(to_h(q_m), to_h(k_m) * MLSTM_HEAD_DIM ** -0.5, to_h(v_m), i_pre, log_f)
    h_m = h_m.transpose(0, 2, 1, 3)
    mu = jnp.mean(h_m, axis=-1, keepdims=True)
    var = jnp.mean(jnp.square(h_m - mu), axis=-1, keepdims=True)
    h_m = ((h_m - mu) * lax.rsqrt(var + EPS)).reshape(B, S, MLSTM_WIDTH)
    h_m = h_m * mlstm_norm.astype(jnp.float32)
    o_m = (h_m.astype(h.dtype) + mlstm_skip * x_conv) * jax.nn.silu(z)

    return jnp.concatenate([o_a, o_m], axis=-1) @ w_out

def second_inputs(seed: int = 0) -> dict:
    key = jax.random.key(seed)
    ks = jax.random.split(key, 32)
    L, D, F = DEPTH_2, D_MODEL, D_FF_2
    H, W, dh = MLSTM_HEADS, MLSTM_WIDTH, MLSTM_HEAD_DIM

    def nrm(k, shape, scale):
        return jax.random.normal(k, shape, jnp.float32) * scale

    b_if = jnp.concatenate([nrm(ks[15], (L, H), 0.1),
                            jnp.broadcast_to(jnp.linspace(3.0, 6.0, H, dtype=jnp.float32), (L, H))
                            + nrm(ks[16], (L, H), 0.1)], axis=-1)
    return {
        'x': nrm(ks[0], (BATCH, SEQ, D), 1.0),
        'c': nrm(ks[1], (BATCH, D), 1.0),
        'w_ada': nrm(ks[2], (L, D, N_MOD * D), 0.2 * D ** -0.5),
        'b_ada': nrm(ks[3], (L, N_MOD * D), 0.02),
        'ffn1_norm': 1.0 + nrm(ks[4], (L, D), 0.02),
        'ffn1_w_gate': nrm(ks[5], (L, D, F), D ** -0.5),
        'ffn1_w_up': nrm(ks[6], (L, D, F), D ** -0.5),
        'ffn1_w_down': nrm(ks[7], (L, F, D), F ** -0.5),
        'mix_norm': 1.0 + nrm(ks[8], (L, D), 0.02),
        'w_in': nrm(ks[9], (L, D, IN_COLS), D ** -0.5),
        'conv_w': nrm(ks[10], (L, CONV_WIDTH, W), CONV_WIDTH ** -0.5),
        'conv_b': nrm(ks[11], (L, W), 0.02),
        'w_q_m': nrm(ks[12], (L, H, dh, dh), dh ** -0.5),
        'w_k_m': nrm(ks[13], (L, H, dh, dh), dh ** -0.5),
        'w_v_m': nrm(ks[14], (L, H, dh, dh), dh ** -0.5),
        'w_if': nrm(ks[17], (L, 3 * W, 2 * H), 0.1 * (3 * W) ** -0.5),
        'b_if': b_if,
        'mlstm_norm': 1.0 + nrm(ks[18], (L, W), 0.02),
        'mlstm_skip': 1.0 + nrm(ks[19], (L, W), 0.02),
        'attn_norm': 1.0 + nrm(ks[20], (L, ATTN_WIDTH), 0.02),
        'w_out': nrm(ks[21], (L, D, D), D ** -0.5),
        'ffn2_norm': 1.0 + nrm(ks[22], (L, D), 0.02),
        'ffn2_w_gate': nrm(ks[23], (L, D, F), D ** -0.5),
        'ffn2_w_up': nrm(ks[24], (L, D, F), D ** -0.5),
        'ffn2_w_down': nrm(ks[25], (L, F, D), F ** -0.5),
        'final_norm': 1.0 + nrm(ks[26], (D,), 0.02),
    }

def second_block(x, c, w_ada, b_ada, ffn1_norm, ffn1_w_gate, ffn1_w_up, ffn1_w_down,
              mix_norm, w_in, conv_w, conv_b, w_q_m, w_k_m, w_v_m, w_if, b_if,
              mlstm_norm, mlstm_skip, attn_norm, w_out,
              ffn2_norm, ffn2_w_gate, ffn2_w_up, ffn2_w_down, final_norm):
    B = x.shape[0]
    for l in range(DEPTH_2):
        mod = (c @ w_ada[l] + b_ada[l]).reshape(B, N_MOD, D_MODEL)
        sh1, sc1, g1, sh2, sc2, g2, sh3, sc3, g3 = [mod[:, None, i] for i in range(N_MOD)]
        h = modulate(rmsnorm_2(x, ffn1_norm[l]), sh1, sc1)
        x = x + 0.5 * (1 + g1) * swiglu_2(h, ffn1_w_gate[l], ffn1_w_up[l], ffn1_w_down[l])
        h = modulate(rmsnorm_2(x, mix_norm[l]), sh2, sc2)
        x = x + (1 + g2) * hybrid_mixer(h, w_in[l], conv_w[l], conv_b[l], w_q_m[l], w_k_m[l],
                                        w_v_m[l], w_if[l], b_if[l], mlstm_norm[l], mlstm_skip[l],
                                        attn_norm[l], w_out[l])
        h = modulate(rmsnorm_2(x, ffn2_norm[l]), sh3, sc3)
        x = x + 0.5 * (1 + g3) * swiglu_2(h, ffn2_w_gate[l], ffn2_w_up[l], ffn2_w_down[l])
    return rmsnorm_2(x, final_norm)


_first_inputs = second_inputs


def second_inputs(seed=0):
    import zlib

    import numpy as np

    out = dict(_first_inputs(seed))
    spreads = {}
    factors = {'ffn1_norm': 5.329,
     'mix_norm': 3.33,
     'conv_b': 4.685,
     'w_if': 2.945,
     'mlstm_norm': 56.2,
     'mlstm_skip': 23.765,
     'attn_norm': 46.352,
     'ffn2_norm': 28.831,
     'final_norm': 7.863}
    for name, (base, spread) in spreads.items():
        noise = np.random.default_rng([zlib.crc32(name.encode()), seed]).standard_normal(out[name].shape)
        drawn = base * np.exp(spread * noise) if base else spread * noise
        out[name] = __import__('jax').numpy.asarray(drawn.astype(out[name].dtype))
    for name, factor in factors.items():
        out[name] = (out[name] * factor).astype(out[name].dtype)
    return out


_narrow_inputs = second_inputs


def second_inputs(seed=0):

    out = dict(_narrow_inputs(seed))
    wider = {'mlstm_norm': 3.69, 'mlstm_skip': 3.53, 'attn_norm': 10.08, 'final_norm': 3.12}
    for name, times in wider.items():
        mean = out[name].mean()
        out[name] = (mean + times * (out[name] - mean)).astype(out[name].dtype)
    return out


DEPTH_3 = 4

SB_HEADS = 16
SB_HEAD_DIM = D_MODEL // SB_HEADS
SB_Q_BLOCK = 128
CONV_WIDTH_3 = 3
GLA_HEADS = 4
GLA_DK = D_MODEL // 2
GLA_DV = D_MODEL
GLA_DK_HEAD = GLA_DK // GLA_HEADS
GLA_DV_HEAD = GLA_DV // GLA_HEADS
GLA_GATE_RANK = 16
GLA_GATE_NORMALIZER = 16.0
GLA_CHUNK = 64
D_FF_3 = 4 * D_MODEL


def rms_norm(x, gain):
    xf = x.astype(jnp.float32)
    y = xf * lax.rsqrt(jnp.mean(xf * xf, axis=-1, keepdims=True) + RMS_EPS) * gain.astype(jnp.float32)
    return y.astype(x.dtype)

def stick_breaking_mixer(xn, w_qkv, w_o):
    b, s, _ = xn.shape
    qkv = (xn @ w_qkv).reshape(b, s, 3, SB_HEADS, SB_HEAD_DIM)
    q, k, v = [qkv[:, :, i].transpose(0, 2, 1, 3).astype(jnp.float32) for i in range(3)]
    scale = SB_HEAD_DIM ** -0.5
    n_blocks = s // SB_Q_BLOCK
    q_blocks = q.reshape(b, SB_HEADS, n_blocks, SB_Q_BLOCK, SB_HEAD_DIM).transpose(2, 0, 1, 3, 4)
    key_pos = jnp.arange(s)

    def one_block(args):
        qb, start = args
        z = jnp.einsum('bhqd,bhkd->bhqk', qb, k) * scale
        q_pos = start + jnp.arange(SB_Q_BLOCK)
        mask = key_pos[None, :] < q_pos[:, None]
        log_beta = jax.nn.log_sigmoid(z)
        log_1m_beta = jnp.where(mask, jax.nn.log_sigmoid(-z), 0.0)
        suffix = lax.cumsum(log_1m_beta, axis=3, reverse=True) - log_1m_beta
        weights = jnp.where(mask, jnp.exp(log_beta + suffix), 0.0)
        return jnp.einsum('bhqk,bhkd->bhqd', weights, v)

    o = lax.map(one_block, (q_blocks, jnp.arange(n_blocks) * SB_Q_BLOCK))
    o = o.transpose(1, 0, 3, 2, 4).reshape(b, s, D_MODEL).astype(xn.dtype)
    return o @ w_o

def short_conv_mixer(xn, w_in, conv_w, w_out):
    s = xn.shape[1]
    bcu = xn @ w_in
    b_gate, c_gate, u = jnp.split(bcu, 3, axis=-1)
    h = c_gate * u
    hp = jnp.pad(h, ((0, 0), (CONV_WIDTH_3 - 1, 0), (0, 0)))
    conv = sum(conv_w[i] * hp[:, i:i + s] for i in range(CONV_WIDTH_3))
    return (b_gate * conv) @ w_out

def gla_mixer(xn, w_in, w_gate_up, b_gate, head_norm, w_o):
    b, s, _ = xn.shape
    n_chunks = s // GLA_CHUNK
    proj = xn @ w_in
    q, k, v, g, a_low = jnp.split(
        proj, np.cumsum([GLA_DK, GLA_DK, GLA_DV, GLA_DV]).tolist(), axis=-1)
    log_gate = jax.nn.log_sigmoid(
        (a_low @ w_gate_up + b_gate).astype(jnp.float32)) / GLA_GATE_NORMALIZER

    def to_chunks(t, dh):
        t = t.astype(jnp.float32).reshape(b, n_chunks, GLA_CHUNK, GLA_HEADS, dh)
        return t.transpose(1, 0, 3, 2, 4)

    qc = to_chunks(q, GLA_DK_HEAD) * (GLA_DK_HEAD ** -0.5)
    kc = to_chunks(k, GLA_DK_HEAD)
    vc = to_chunks(v, GLA_DV_HEAD)
    gc = to_chunks(log_gate, GLA_DK_HEAD)
    causal = jnp.tril(jnp.ones((GLA_CHUNK, GLA_CHUNK), dtype=bool))

    def step(state, inp):
        qi, ki, vi, gi = inp
        cum = jnp.cumsum(gi, axis=2)
        inter = jnp.einsum('bhcd,bhde->bhce', qi * jnp.exp(cum), state)
        diff = cum[:, :, :, None, :] - cum[:, :, None, :, :]
        decay = jnp.exp(jnp.where(causal[None, None, :, :, None], diff, -jnp.inf))
        scores = jnp.einsum('bhid,bhjd,bhijd->bhij', qi, ki, decay)
        out = inter + jnp.einsum('bhij,bhje->bhie', scores, vi)
        last = cum[:, :, -1:, :]
        new_state = jnp.exp(last)[:, :, 0, :, None] * state + jnp.einsum(
            'bhcd,bhce->bhde', ki * jnp.exp(last - cum), vi)
        return new_state, out

    state0 = jnp.zeros((b, GLA_HEADS, GLA_DK_HEAD, GLA_DV_HEAD), jnp.float32)
    _, o = lax.scan(step, state0, (qc, kc, vc, gc))
    o = o.transpose(1, 0, 3, 2, 4).reshape(b, s, GLA_HEADS, GLA_DV_HEAD)
    o = rms_norm(o, head_norm).reshape(b, s, GLA_DV).astype(xn.dtype)
    return (o * jax.nn.silu(g)) @ w_o

def squared_relu_mlp(xn, w_up, w_down):
    return jnp.square(jax.nn.relu(xn @ w_up)) @ w_down

def third_inputs(seed: int = 0) -> dict:
    key = jax.random.key(seed)
    ks = jax.random.split(key, 16)
    n_sb = (DEPTH_3 + 2) // 3
    n_conv = (DEPTH_3 + 1) // 3
    n_gla = DEPTH_3 // 3
    f32 = jnp.float32

    def nrm(k, shape, scale):
        return jax.random.normal(k, shape, f32) * scale

    d_in_gla = 2 * GLA_DK + 2 * GLA_DV + GLA_GATE_RANK
    return {
        "x": nrm(ks[0], (BATCH, SEQ, D_MODEL), 1.0),
        "norm_gains": 1.0 + nrm(ks[1], (DEPTH_3, 4, D_MODEL), 0.02),
        "sb_w_qkv": nrm(ks[2], (n_sb, D_MODEL, 3 * D_MODEL), D_MODEL ** -0.5),
        "sb_w_o": nrm(ks[3], (n_sb, D_MODEL, D_MODEL), D_MODEL ** -0.5),
        "conv_w_in": nrm(ks[4], (n_conv, D_MODEL, 3 * D_MODEL), D_MODEL ** -0.5),
        "conv_w": nrm(ks[5], (n_conv, CONV_WIDTH_3, D_MODEL), CONV_WIDTH_3 ** -0.5),
        "conv_w_out": nrm(ks[6], (n_conv, D_MODEL, D_MODEL), D_MODEL ** -0.5),
        "gla_w_in": nrm(ks[7], (n_gla, D_MODEL, d_in_gla), D_MODEL ** -0.5),
        "gla_w_gate_up": nrm(ks[8], (n_gla, GLA_GATE_RANK, GLA_DK), GLA_GATE_RANK ** -0.5),
        "gla_b_gate": nrm(ks[9], (n_gla, GLA_DK), 0.1),
        "gla_head_norm": 1.0 + nrm(ks[10], (n_gla, GLA_HEADS, GLA_DV_HEAD), 0.02),
        "gla_w_o": nrm(ks[11], (n_gla, GLA_DV, D_MODEL), GLA_DV ** -0.5),
        "ffn_w_up": nrm(ks[12], (DEPTH_3, D_MODEL, D_FF_3), D_MODEL ** -0.5),
        "ffn_w_down": nrm(ks[13], (DEPTH_3, D_FF_3, D_MODEL), D_FF_3 ** -0.5),
    }

def third_block(x, norm_gains, sb_w_qkv, sb_w_o, conv_w_in, conv_w, conv_w_out,
              gla_w_in, gla_w_gate_up, gla_b_gate, gla_head_norm, gla_w_o,
              ffn_w_up, ffn_w_down):
    h = x
    for i in range(DEPTH_3):
        kind, j = i % N_MIXERS, i // N_MIXERS
        xn = rms_norm(h, norm_gains[i, 0])
        if kind == 0:
            m = stick_breaking_mixer(xn, sb_w_qkv[j], sb_w_o[j])
        elif kind == 1:
            m = short_conv_mixer(xn, conv_w_in[j], conv_w[j], conv_w_out[j])
        else:
            m = gla_mixer(xn, gla_w_in[j], gla_w_gate_up[j], gla_b_gate[j],
                          gla_head_norm[j], gla_w_o[j])
        h = h + rms_norm(m, norm_gains[i, 1])
        f = squared_relu_mlp(rms_norm(h, norm_gains[i, 2]), ffn_w_up[i], ffn_w_down[i])
        h = h + rms_norm(f, norm_gains[i, 3])
    return h


def setup_inputs(seed=0):
    out = dict(first_inputs(seed))
    for name, value in second_inputs(seed + 1).items():
        if name != "x":
            out[name + "_2"] = value
    for name, value in third_inputs(seed + 2).items():
        if name != "x":
            out[name + "_3"] = value
    return out


def reference(
    x, ffn1_norm, ffn1_w_gu, ffn1_w_down, mix_norm, ffn2_norm, ffn2_w_gu, ffn2_w_down, nsa_w_in,
    nsa_ck_pe, nsa_ck_w1, nsa_ck_w2, nsa_cv_pe, nsa_cv_w1, nsa_cv_w2, nsa_w_out, swa_w_in,
    swa_sinks, swa_w_out, fox_w_in, fox_b_f, fox_w_out, final_norm, c_2, w_ada_2, b_ada_2,
    ffn1_norm_2, ffn1_w_gate_2, ffn1_w_up_2, ffn1_w_down_2, mix_norm_2, w_in_2, conv_w_2,
    conv_b_2, w_q_m_2, w_k_m_2, w_v_m_2, w_if_2, b_if_2, mlstm_norm_2, mlstm_skip_2,
    attn_norm_2, w_out_2, ffn2_norm_2, ffn2_w_gate_2, ffn2_w_up_2, ffn2_w_down_2, final_norm_2,
    norm_gains_3, sb_w_qkv_3, sb_w_o_3, conv_w_in_3, conv_w_3, conv_w_out_3, gla_w_in_3,
    gla_w_gate_up_3, gla_b_gate_3, gla_head_norm_3, gla_w_o_3, ffn_w_up_3, ffn_w_down_3,
):
    x = first_block(
        x, ffn1_norm, ffn1_w_gu, ffn1_w_down, mix_norm, ffn2_norm, ffn2_w_gu, ffn2_w_down,
        nsa_w_in, nsa_ck_pe, nsa_ck_w1, nsa_ck_w2, nsa_cv_pe, nsa_cv_w1, nsa_cv_w2, nsa_w_out,
        swa_w_in, swa_sinks, swa_w_out, fox_w_in, fox_b_f, fox_w_out, final_norm,
    )
    x = second_block(
        x, c_2, w_ada_2, b_ada_2, ffn1_norm_2, ffn1_w_gate_2, ffn1_w_up_2, ffn1_w_down_2,
        mix_norm_2, w_in_2, conv_w_2, conv_b_2, w_q_m_2, w_k_m_2, w_v_m_2, w_if_2, b_if_2,
        mlstm_norm_2, mlstm_skip_2, attn_norm_2, w_out_2, ffn2_norm_2, ffn2_w_gate_2,
        ffn2_w_up_2, ffn2_w_down_2, final_norm_2,
    )
    return third_block(
        x, norm_gains_3, sb_w_qkv_3, sb_w_o_3, conv_w_in_3, conv_w_3, conv_w_out_3, gla_w_in_3,
        gla_w_gate_up_3, gla_b_gate_3, gla_head_norm_3, gla_w_o_3, ffn_w_up_3, ffn_w_down_3,
    )


_drawn_inputs = setup_inputs


def setup_inputs(seed=0):
    import zlib

    import numpy as np

    out = dict(_drawn_inputs(seed))
    spreads = {}
    factors = {'nsa_ck_pe': 2.844,
     'norm_gains_3': 4.643,
     'gla_w_gate_up_3': 3.509,
     'gla_b_gate_3': 8.0,
     'gla_head_norm_3': 8.0}
    for name, (base, spread) in spreads.items():
        noise = np.random.default_rng([zlib.crc32(name.encode()), seed]).standard_normal(out[name].shape)
        drawn = base * np.exp(spread * noise) if base else spread * noise
        out[name] = jnp.asarray(drawn.astype(out[name].dtype))
    for name, factor in factors.items():
        out[name] = (out[name] * factor).astype(out[name].dtype)
    return out
```

```python
from contextlib import ExitStack

import numpy as np

import concourse.bass as bass
from concourse import mybir
from concourse.alu_op_type import AluOpType as ALU

F32 = mybir.dt.float32
F32R = mybir.dt.float32r
ACT = mybir.ActivationFunctionType
AX = mybir.AxisListType

P = 128
TOKENS = 256
TT = TOKENS // P
D = 1024
KC = D // P
HEAD = 64
HEADS = D // HEAD
D_FF = 2816
D_FF_3 = 4096
EPS = 1e-6
NEG = -1e30
BLK = 512
RING = 2
ARENA = 18432
PROJ_COLS = 3088
UNIT = 2048


def rope_rows():
    inv = np.float32(10000.0) ** (-np.arange(0, HEAD, 2, dtype=np.float32) / HEAD)
    ang = np.arange(TOKENS, dtype=np.float32)[:, None] * inv[None, :].astype(np.float32)
    cos, sin = np.cos(ang), np.sin(ang)
    full = np.concatenate([cos, cos], 1)
    sgn = np.concatenate([-sin, sin], 1)
    f = lambda a: a.reshape(TT, P, HEAD).transpose(1, 0, 2).reshape(P, TT * HEAD)
    return f(full), f(sgn)


CMP_LEN, CMP_STRIDE = 32, 16
CMP_N = (TOKENS - CMP_LEN) // CMP_STRIDE + 1
LEVELS = [2, 4, 8, 16, 32, 64, 128]


def constant_table():
    i = np.arange(P)
    row, col = i[:, None], i[None, :]
    t = {}
    t["ident"] = np.eye(P)
    t["ones"] = np.ones((P, TOKENS))
    causal = np.where(col <= row, 0.0, NEG)
    t["causal"] = np.concatenate([causal, np.zeros((P, P)), causal], 1)
    t["window"] = np.concatenate([causal, np.where(col > row, 0.0, NEG), causal], 1)
    t["before01"] = (row < col) * 1.0
    t["beforeadd"] = np.where(row < col, 0.0, NEG)
    t["causalT"] = np.where(row <= col, 0.0, NEG)
    t["minus_tri"] = (row >= col) * -1.0
    t["minus_ones"] = -np.ones((P, P))
    for b in LEVELS:
        same = (row // b) == (col // b)
        t[f"level{b}"] = (same & (row % b < b // 2) & (col % b >= b // 2)) * 1.0
    t["cos"], t["sin"] = rope_rows()
    tok = np.arange(TOKENS).reshape(TT, P).T[:, :, None]
    ok = (np.arange(CMP_N) * CMP_STRIDE + CMP_LEN - 1)[None, None, :] <= tok
    t["cmp01"] = (ok * 1.0).reshape(P, -1)
    t["cmpadd"] = np.where(ok, 0.0, NEG).reshape(P, -1)
    sel = np.zeros((P, 4, P))
    for h in range(4):
        sel[h, h, :] = 1.0
    t["rowsel"] = sel.reshape(P, -1)
    return {k: np.asarray(v, np.float32) for k, v in t.items()}


CONST_COLS = {}
_at = 0
for _k, _v in constant_table().items():
    CONST_COLS[_k] = (_at, _v.shape[1])
    _at += _v.shape[1]
CONST_N = _at

COLUMN_VECTORS = (
    [(f"{n}{l}", D) for n in ("ffn1_norm", "mix_norm", "ffn2_norm") for l in range(2)]
    + [(n, D) for n in ("ffn1_norm_2", "mix_norm_2", "ffn2_norm_2")]
    + [(f"norm_gains_3_{i}{j}", D) for i in range(4) for j in (0, 2)]
    + [(f"conv_w_2_{i}", 512) for i in range(4)] + [("conv_b_2", 512)]
    + [("mlstm_norm_2", 512), ("mlstm_skip_2", 512), ("attn_norm_2", 512)]
    + [(f"conv_w_3_{i}", D) for i in range(3)]
    + [("gla_head_norm_3", D), ("gla_b_gate_3", 512)]
    + [("c_2", D)]
    + [("ck_pe", 2048), ("cv_pe", 2048)]
)
COL_AT = {}
_at = 0
for _k, _n in COLUMN_VECTORS:
    COL_AT[_k] = (_at, _n // P)
    _at += _n // P
COL_N = _at
ROW_VECTORS = ["final_norm", "final_norm_2"] + [f"norm_gains_3_{i}{j}" for i in range(4) for j in (1, 3)]


class Signal:

    def __init__(self, sem):
        self.sem, self.planned = sem, 0

    def plan(self, n):
        base = self.planned
        self.planned += n
        return base


def wait_all(eng, pairs):
    for sem, value in pairs:
        if value > 0:
            eng.wait_ge(sem, value)


class Core:

    def __init__(self, nc, ctx, dram):
        self.nc, self.dram = nc, dram

        def sb(name, *shape):
            return ctx.enter_context(nc.sbuf_tensor(name, [P, *shape], F32))

        def sig(name):
            return Signal(ctx.enter_context(nc.semaphore(name)))

        def split(name, *shape):
            return ctx.enter_context(nc.sbuf_tensor(name, [P, *shape], F32R))

        self.sb, self.sig = sb, sig
        self.const = sb("const", CONST_N)
        self.cols = sb("cols", COL_N)
        self.x = sb("x", TT, D)
        self.y = sb("y", TT, D)
        self.feat_hi = split("feat_hi", KC, TOKENS)
        self.feat_lo = split("feat_lo", KC, TOKENS)
        self.in_hi = split("in_hi", RING, UNIT)
        self.in_lo = split("in_lo", RING, UNIT)
        self.ring_in = sb("ring_in", RING, UNIT)
        self.act = sb("act", RING, 2 * TOKENS)
        self.small = sb("small", 64)
        self.row = sb("row", D)
        self.minus_half = sb("minus_half", 8)
        at = nc.sbuf_base
        self.proj = sb("proj", TT, PROJ_COLS)

        def placed(name, offset, dtype, *shape):
            return nc.alloc_sbuf_tensor_at(name, [P, *shape], dtype, offset=offset)

        self.ring_down = placed("ring_down", at, F32, RING, UNIT)
        at += 4 * RING * UNIT
        self.hid_hi = placed("hid_hi", at, F32R, RING, 2 * TOKENS)
        at += 4 * RING * 2 * TOKENS
        self.hid_lo = placed("hid_lo", at, F32R, RING, 2 * TOKENS)
        at = nc.sbuf_base
        self.arena = sb("arena", ARENA)
        self.down_hi = placed("down_hi", at, F32R, RING, UNIT)
        at += 4 * RING * UNIT
        self.down_lo = placed("down_lo", at, F32R, RING, UNIT)
        at += 4 * RING * UNIT
        self.mod_sum = placed("mod_sum", at, F32, 3, D)
        at += 4 * 3 * D
        self.mod_w = placed("mod_w", at, F32, 2, D)
        self.bank = [ctx.enter_context(nc.psum_tensor(f"bank{i}", [P, 512], F32)) for i in range(6)]
        spare = ctx.enter_context(nc.psum_tensor("spare", [P, 1024], F32))
        self.bank += [spare[:, 0:512], spare[:, 512:1024]]
        self.spare = spare
        self.in_landed = [sig(f"in_landed{i}") for i in range(RING)]
        self.down_landed = [sig(f"down_landed{i}") for i in range(RING)]
        self.in_hi_ready = sig("in_hi_ready")
        self.in_lo_ready = sig("in_lo_ready")
        self.down_hi_ready = sig("down_hi_ready")
        self.down_lo_ready = sig("down_lo_ready")
        self.in_used = sig("in_used")
        self.down_used = sig("down_used")
        self.raw_ready = sig("raw_ready")
        self.hid_hi_ready = sig("hid_hi_ready")
        self.turn_hi = sig("turn_hi")
        self.turn_lo = sig("turn_lo")
        self.consts_landed = sig("consts_landed")
        self.in_units = 0
        self.down_units = 0
        self.gu_ready = sig("gu_ready")
        self.act_ready = sig("act_ready")
        self.hid_ready = sig("hid_ready")
        self.acc_ready = sig("acc_ready")
        self.acc_read_act = sig("acc_read_act")
        self.acc_read_dve = sig("acc_read_dve")
        self.squares_ready = sig("squares_ready")
        self.rstd_ready = sig("rstd_ready")
        self.normed_act = sig("normed_act")
        self.normed_dve = sig("normed_dve")
        self.row_landed = sig("row_landed")
        self.turned = sig("turned")
        self.turn_read_act = sig("turn_read_act")
        self.turn_read_dve = sig("turn_read_dve")
        self.dve_step = sig("dve_step")
        self.act_step = sig("act_step")
        self.pool_step = sig("pool_step")
        self.dve_n = self.act_n = self.pool_n = 0
        more_signals(self)

    def c(self, name, lo=0, hi=None):
        at, n = CONST_COLS[name]
        return self.const[:, at + lo:at + (n if hi is None else hi)]

    def bank_tiles(self, i):
        return self.bank[i][:, :].rearrange("p (t n) -> p t n", t=TT)

    def col(self, name, chunk, n=1):
        at, _ = COL_AT[name]
        return self.cols[:, at + chunk:at + chunk + n]

    def dve_link(self, dve, ins):
        self.dve_n += 1
        ins.then_inc(self.dve_step.sem, 1)
        dve.wait_ge(self.dve_step.sem, self.dve_n)

    def act_link(self, act, ins):
        self.act_n += 1
        ins.then_inc(self.act_step.sem, 1)
        act.wait_ge(self.act_step.sem, self.act_n)

    def pool_link(self, pool, ins):
        self.pool_n += 1
        ins.then_inc(self.pool_step.sem, 1)
        pool.wait_ge(self.pool_step.sem, self.pool_n)


class Stage:

    def __init__(self, core, before):
        self.k, self.before = core, before.done if before else []
        self.done = self.before

    def tensor(self, pe):
        pass

    def scalar(self, act):
        pass

    def vector(self, dve):
        pass

    def gpsimd(self, pool):
        pass

    def sync(self, sp):
        pass


def split_hi(k, act, landed, used, hi_ready, raw, hi, g, m, n):
    s = g % RING
    act.wait_ge(landed[s].sem, m * (16 // RING) + 16 * (g // RING + 1))
    if not isinstance(m, int) or g + m >= RING:
        act.wait_ge(used.sem, m + g - RING + 1)
    act.copy(hi[:, s, 0:n], raw[:, s, 0:n]).then_inc(hi_ready.sem, 1)


def split_lo(k, dve, hi_ready, lo_ready, raw, hi, lo, g, m, n):
    s = g % RING
    dve.wait_ge(hi_ready.sem, m + g + 1)
    dve.tensor_tensor(lo[:, s, 0:n], raw[:, s, 0:n], hi[:, s, 0:n].bitcast(F32), ALU.subtract).then_inc(lo_ready.sem, 1)


def in_hi(k, act, g, m=0):
    split_hi(k, act, k.in_landed, k.in_used, k.in_hi_ready, k.ring_in, k.in_hi, g, m, UNIT)


def in_lo(k, dve, g, m=0):
    split_lo(k, dve, k.in_hi_ready, k.in_lo_ready, k.ring_in, k.in_hi, k.in_lo, g, m, UNIT)


class Presplit(Stage):

    def __init__(self, core, before):
        super().__init__(core, before)
        self.u0 = core.in_units

    def scalar(self, act):
        for i in range(RING):
            in_hi(self.k, act, self.u0 + i)

    def vector(self, dve):
        for i in range(RING):
            in_lo(self.k, dve, self.u0 + i)


class Load(Stage):

    def __init__(self, core, before=None):
        super().__init__(core, before)
        core.consts_landed.plan(48)
        self.done = [(core.consts_landed.sem, 48)]

    def gpsimd(self, pool):
        k = self.k
        k.pool_link(pool, pool.memset(k.minus_half[:], -0.5))

    def sync(self, sp):
        k = self.k
        s = k.consts_landed.sem
        sp.dma_start(k.x[:], k.dram["x"].rearrange("(t p) d -> p t d", p=P)).then_inc(s, 16)
        sp.dma_start(k.const[:], k.dram["const"]).then_inc(s, 16)
        sp.dma_start(k.cols[:], k.dram["cols"]).then_inc(s, 16)


class Store(Stage):
    def __init__(self, core, before):
        super().__init__(core, before)
        self.stored = core.sig("stored")

    def sync(self, sp):
        wait_all(sp, self.before)
        sp.dma_start(self.k.dram["out"].rearrange("(t p) d -> p t d", p=P), self.k.x[:]).then_inc(self.stored.sem, 16)
        sp.wait_ge(self.stored.sem, 16)


class Turn(Stage):

    def __init__(self, core, before, src, dst, chunks, scale=None, shift=None):
        super().__init__(core, before)
        self.src, self.dst, self.chunks, self.scale, self.shift = src, dst, chunks, scale, shift
        assert chunks % 2 == 0
        self.banks = chunks // 2
        self.t0 = core.turned.plan(self.banks)
        self.a0 = core.turn_read_act.plan((self.banks + 1) // 2)
        self.d0 = core.turn_read_dve.plan(self.banks // 2)
        self.done = [(core.turn_read_act.sem, self.a0 + (self.banks + 1) // 2),
                     (core.turn_read_dve.sem, self.d0 + self.banks // 2)]

    def tensor(self, pe):
        k = self.k
        wait_all(pe, self.before)
        for b in range(self.banks):
            if b >= 4:
                if b % 2 == 0:
                    pe.wait_ge(k.turn_read_act.sem, self.a0 + b // 2 - 1)
                else:
                    pe.wait_ge(k.turn_read_dve.sem, self.d0 + b // 2 - 1)
            for j in range(2):
                for t in range(TT):
                    last = pe.transpose(k.bank[b % 4][:, (j * TT + t) * P:(j * TT + t + 1) * P],
                                        self.src(t, 2 * b + j), k.c("ident"))
            last.then_inc(k.turned.sem, 1)

    def _read(self, eng, is_act, b):
        k = self.k
        if self.scale is None:
            out = self.dst[:, 2 * b:2 * b + 2, :].rearrange("p c n -> p (c n)")
            return (eng.copy if is_act else eng.tensor_copy)(out, k.bank[b % 4][:])
        for j in range(2):
            c = 2 * b + j
            out, src = self.dst[:, c, :], k.bank[b % 4][:, j * TOKENS:(j + 1) * TOKENS]
            if is_act:
                if self.shift is None:
                    last = eng.activation(out, src, ACT.Copy, scale=self.scale(c))
                else:
                    last = eng.activation(out, src, ACT.Identity, bias=self.shift(c), scale=self.scale(c))
            elif self.shift is None:
                last = eng.tensor_scalar(out, src, self.scale(c), None, ALU.mult)
            else:
                last = eng.tensor_scalar(out, src, self.scale(c), self.shift(c), ALU.mult, ALU.add)
        return last

    def scalar(self, act):
        wait_all(act, self.before)
        for b in range(0, self.banks, 2):
            act.wait_ge(self.k.turned.sem, self.t0 + b + 1)
            self._read(act, True, b).then_inc(self.k.turn_read_act.sem, 1)

    def vector(self, dve):
        wait_all(dve, self.before)
        for b in range(1, self.banks, 2):
            dve.wait_ge(self.k.turned.sem, self.t0 + b + 1)
            self._read(dve, False, b).then_inc(self.k.turn_read_dve.sem, 1)


class FeatTurn(Stage):

    def __init__(self, core, before, src, scale=None, shift=None, tmp=None):
        super().__init__(core, before)
        self.src, self.scale, self.shift = src, scale, shift
        self.banks = KC // 2
        self.t0, self.h0, self.l0 = core.turned.plan(self.banks), core.turn_hi.plan(self.banks), core.turn_lo.plan(self.banks)
        self.done = [(core.turn_lo.sem, self.l0 + self.banks)]

    def tensor(self, pe):
        k = self.k
        wait_all(pe, self.before)
        for b in range(self.banks):
            for j in range(2):
                for t in range(TT):
                    last = pe.transpose(k.bank[b][:, (j * TT + t) * P:(j * TT + t + 1) * P], self.src(t, 2 * b + j), k.c("ident"))
            last.then_inc(k.turned.sem, 1)

    def scalar(self, act):
        k = self.k
        wait_all(act, self.before)
        for b in range(self.banks):
            act.wait_ge(k.turned.sem, self.t0 + b + 1)
            if self.scale is None:
                last = act.copy(k.feat_hi[:, 2 * b:2 * b + 2, :].rearrange("p c n -> p (c n)"), k.bank[b][:])
            else:
                for c in (2 * b, 2 * b + 1):
                    out, src = k.feat_hi[:, c, :], k.bank[b][:, (c % 2) * TOKENS:(c % 2 + 1) * TOKENS]
                    if self.shift is None:
                        last = act.activation(out, src, ACT.Copy, scale=self.scale(c))
                    else:
                        last = act.activation(out, src, ACT.Identity, bias=self.shift(c), scale=self.scale(c))
            last.then_inc(k.turn_hi.sem, 1)

    def vector(self, dve):
        k = self.k
        wait_all(dve, self.before)
        for b in range(self.banks):
            dve.wait_ge(k.turn_hi.sem, self.h0 + b + 1)
            if self.scale is None:
                last = dve.tensor_tensor(k.feat_lo[:, 2 * b:2 * b + 2, :].rearrange("p c n -> p (c n)"), k.bank[b][:],
                                         k.feat_hi[:, 2 * b:2 * b + 2, :].rearrange("p c n -> p (c n)").bitcast(F32), ALU.subtract)
            else:
                for c in (2 * b, 2 * b + 1):
                    out, src = k.feat_lo[:, c, :], k.bank[b][:, (c % 2) * TOKENS:(c % 2 + 1) * TOKENS]
                    hi = k.feat_hi[:, c, :].bitcast(F32)
                    if self.shift is None:
                        last = dve.scalar_tensor_tensor(out, src, self.scale(c), hi, ALU.mult, ALU.subtract)
                    else:
                        whole = k.act[:, c % 2, 0:TOKENS]
                        k.dve_link(dve, dve.tensor_scalar(whole, src, self.scale(c), self.shift(c), ALU.mult, ALU.add))
                        last = dve.tensor_tensor(out, whole, hi, ALU.subtract)
            last.then_inc(k.turn_lo.sem, 1)


def feat_from(k, dve, value, lo_chunk, hi_chunk):
    hi, lo = k.feat_hi[:, lo_chunk:hi_chunk, :], k.feat_lo[:, lo_chunk:hi_chunk, :]
    k.dve_link(dve, dve.tensor_copy(hi, value))
    return dve.tensor_tensor(lo, value, hi.bitcast(F32), ALU.subtract)


class Rstd(Stage):

    def __init__(self, core, before, src, groups, width, out=None, row=None, add_to=None):
        super().__init__(core, before)
        self.src, self.groups, self.width, self.out = src, groups, width, out
        self.row, self.add_to = row, add_to
        self.s0 = core.squares_ready.plan(1)
        self.r0 = core.rstd_ready.plan(1)
        self.n0 = core.normed_dve.plan(groups)
        self.done = [(core.normed_dve.sem, self.n0 + groups)]
        if row is not None:
            self.l0 = core.row_landed.plan(16)

    def scalar(self, act):
        k = self.k
        wait_all(act, self.before)
        for g in range(self.groups):
            if g:
                k.act_link(act, last)
            last = act.activation(k.spare[:, 0:self.width], self.src(g), ACT.Square, accum_out=k.small[:, g:g + 1])
        last.then_inc(k.squares_ready.sem, 1)

    def gpsimd(self, pool):
        k, n = self.k, self.groups
        wait_all(pool, self.before)
        if self.row is not None:
            pool.dma_start(k.row[:], k.dram["rows"][self.row:self.row + 1, :].partition_broadcast(P)).then_inc(k.row_landed.sem, 16)
        pool.wait_ge(k.squares_ready.sem, self.s0 + 1)
        k.pool_link(pool, pool.tensor_scalar(k.small[:, 8:8 + n], k.small[:, 0:n], 1.0 / self.width, EPS, ALU.mult, ALU.add))
        pool.tensor_tensor(k.small[:, 16:16 + n], k.small[:, 8:8 + n], k.minus_half[:, 0:n], ALU.pow).then_inc(k.rstd_ready.sem, 1)

    def vector(self, dve):
        k = self.k
        wait_all(dve, self.before)
        dve.wait_ge(k.rstd_ready.sem, self.r0 + 1)
        if self.row is not None:
            dve.wait_ge(k.row_landed.sem, self.l0 + 16)
        for g in range(self.groups):
            rstd = k.small[:, 16 + g:17 + g]
            if self.row is None:
                dve.tensor_scalar(self.out(g), self.src(g), rstd, None, ALU.mult).then_inc(k.normed_dve.sem, 1)
            elif self.add_to is None:
                dve.scalar_tensor_tensor(self.out(g), self.src(g), rstd, k.row[:], ALU.mult, ALU.mult).then_inc(k.normed_dve.sem, 1)
            else:
                k.dve_link(dve, dve.scalar_tensor_tensor(self.src(g), self.src(g), rstd, k.row[:], ALU.mult, ALU.mult))
                dve.tensor_tensor(self.add_to(g), self.add_to(g), self.src(g), ALU.add).then_inc(k.normed_dve.sem, 1)


def pre_norm(core, before, gain, scale=None, shift=None):
    early = Presplit(core, before)
    r = Rstd(core, early, lambda g: core.x[:, g, :], TT, D, out=lambda g: core.y[:, g, :])
    t = FeatTurn(core, r, lambda t, c: core.y[:, t, c * P:(c + 1) * P], scale or (lambda c: core.col(gain, c)), shift)
    return [early, r, t]


def row_norm(core, before, row):
    return [Rstd(core, before, lambda g: core.x[:, g, :], TT, D, out=lambda g: core.x[:, g, :], row=ROW_VECTORS.index(row))]


def post_norm(core, before, row):
    return [Rstd(core, before, lambda g: core.y[:, g, :], TT, D, row=ROW_VECTORS.index(row), add_to=lambda g: core.x[:, g, :])]


def read_out(k, dve, acc, t, cols, how):
    lo, hi = cols
    x = k.x[:, t, lo:hi]
    if how == "half":
        return dve.scalar_tensor_tensor(x, acc, 0.5, x, ALU.mult, ALU.add)
    if how == "add":
        return dve.tensor_tensor(x, acc, x, ALU.add)
    if how == "y":
        return dve.tensor_copy(k.y[:, t, lo:hi], acc)
    k.dve_link(dve, dve.tensor_tensor(k.y[:, t, lo:hi], acc, how[:, lo:hi], ALU.mult))
    return dve.tensor_tensor(x, x, k.y[:, t, lo:hi], ALU.add)


class FeedForward(Stage):

    def __init__(self, core, before, w_in, w_down, silu, how):
        super().__init__(core, before)
        self.w_in, self.w_down, self.silu, self.how = core.dram[w_in], core.dram[w_down], silu, how
        self.chunks = 1 if silu else 2
        self.units = (D_FF if silu else D_FF_3) // (P * self.chunks)
        assert self.units % 2 == 0
        n = self.units
        self.u0, self.w0 = core.in_units, core.down_units
        core.in_units += n
        core.down_units += n
        self.gu0, self.ac0, self.hd0 = core.gu_ready.plan(n), core.act_ready.plan(n), core.hid_ready.plan(n)
        self.ar0 = core.acc_ready.plan(1)
        self.rd0 = core.acc_read_dve.plan(4)
        self.done = [(core.acc_read_dve.sem, self.rd0 + 4)]

    def _load_in(self, sp, m, j):
        k, g = self.k, self.u0 + j
        s = g % RING
        if not isinstance(m, int) or g + m >= RING:
            sp.wait_ge(k.in_lo_ready.sem, m + g - RING + 1)
        sp.dma_start(k.ring_in[:, s, :], self.w_in[bass.ds(m + j, 1)].rearrange("a p n -> p (a n)")).then_inc(k.in_landed[s].sem, 16)

    def _load_down(self, sp, m, j):
        k, g = self.k, self.w0 + j
        s = g % RING
        if not isinstance(m, int) or g + m >= RING:
            sp.wait_ge(k.down_lo_ready.sem, m + g - RING + 1)
        sp.dma_start(k.ring_down[:, s, 0:self.chunks * D],
                     self.w_down[bass.ds(m + j, 1)].rearrange("a p n -> p (a n)")).then_inc(k.down_landed[s].sem, 16)

    def sync(self, sp):
        self._load_in(sp, 0, 0)
        self._load_in(sp, 0, 1)
        wait_all(sp, self.before)
        self._load_down(sp, 0, 0)
        self._load_down(sp, 0, 1)
        with sp.Fori(1, self.units // 2) as turn:
            i = turn * 2
            for j in range(2):
                self._load_in(sp, i, j)
                self._load_down(sp, i, j)

    def _hidden(self, pe, m, j):
        k = self.k
        s, g = (self.u0 + j) % RING, self.u0 + j
        pe.wait_ge(k.in_lo_ready.sem, m + g + 1)
        if not isinstance(m, int) or m + j >= 2:
            pe.wait_ge(k.raw_ready.sem, m + (self.hd0 + j - 1))
        for h in range(2):
            out = k.bank[4 + j][:, h * TOKENS:(h + 1) * TOKENS]
            for c in range(KC):
                w = slice((h * KC + c) * P, (h * KC + c + 1) * P)
                hi, lo = k.in_hi[:, s, w], k.in_lo[:, s, w]
                pe.matmul(out, hi, k.feat_hi[:, c, :], start=(c == 0), stop=False)
                pe.matmul(out, hi, k.feat_lo[:, c, :], start=False, stop=False)
                last = pe.matmul(out, lo, k.feat_hi[:, c, :], start=False, stop=(c == KC - 1))
        last.then_inc(k.in_used.sem, 1)

    def _down(self, pe, m, j, first, final):
        k = self.k
        s, g = (self.w0 + j) % RING, self.w0 + j
        pe.wait_ge(k.down_lo_ready.sem, m + g + 1)
        pe.wait_ge(k.hid_ready.sem, m + (self.hd0 + j + 1))
        for ch in range(self.chunks):
            for t in range(TT):
                rows = slice(ch * TOKENS + t * P, ch * TOKENS + (t + 1) * P)
                for n in range(D // BLK):
                    cols = slice(ch * D + n * BLK, ch * D + (n + 1) * BLK)
                    out = k.bank[t * 2 + n][:]
                    opens, closes = first and ch == 0, final and ch == self.chunks - 1
                    pe.matmul(out, k.hid_hi[:, j, rows], k.down_hi[:, s, cols], start=opens, stop=False)
                    pe.matmul(out, k.hid_hi[:, j, rows], k.down_lo[:, s, cols], start=False, stop=False)
                    last = pe.matmul(out, k.hid_lo[:, j, rows], k.down_hi[:, s, cols], start=False, stop=closes)
        last.then_inc(k.down_used.sem, 1)

    def tensor(self, pe):
        wait_all(pe, self.before)
        self._hidden(pe, 0, 0)
        self._hidden(pe, 0, 1)
        self._down(pe, 0, 0, True, False)
        with pe.Fori(1, self.units // 2) as turn:
            i = turn * 2
            self._hidden(pe, i, 0)
            self._down(pe, i - 2, 1, False, False)
            self._hidden(pe, i, 1)
            self._down(pe, i, 0, False, False)
        self._down(pe, self.units - 2, 1, False, True)

    def _down_hi(self, act, m, j):
        k = self.k
        split_hi(k, act, k.down_landed, k.down_used, k.down_hi_ready, k.ring_down, k.down_hi, self.w0 + j, m, self.chunks * D)

    def _down_lo(self, dve, m, j):
        k = self.k
        split_lo(k, dve, k.down_hi_ready, k.down_lo_ready, k.ring_down, k.down_hi, k.down_lo, self.w0 + j, m, self.chunks * D)

    def _activate(self, act, m, j):
        k, n = self.k, TOKENS if self.silu else 2 * TOKENS
        act.wait_ge(k.in_used.sem, m + (self.u0 + j + 1))
        if not isinstance(m, int) or m + j >= 2:
            act.wait_ge(k.hid_ready.sem, m + (self.hd0 + j - 1))
        act.activation(k.act[:, j, 0:n], k.bank[4 + j][:, 0:n], ACT.Silu if self.silu else ACT.Relu).then_inc(k.act_ready.sem, 1)

    def _units(self, eng, split_in, split_down, use):
        def unit(m, j, more):
            if more:
                split_in(self.k, eng, self.u0 + j + 1, m)
            split_down(eng, m, j)
            use(eng, m, j)
        unit(0, 0, False)
        unit(0, 1, True)
        with eng.Fori(1, self.units // 2 - 1) as turn:
            i = turn * 2
            unit(i, 0, True)
            unit(i, 1, True)
        unit(self.units - 2, 0, True)
        unit(self.units - 2, 1, False)

    def scalar(self, act):
        wait_all(act, self.before)
        self._units(act, in_hi, self._down_hi, self._activate)

    def _multiply(self, dve, m, j):
        k, n = self.k, TOKENS if self.silu else 2 * TOKENS
        dve.wait_ge(k.act_ready.sem, m + (self.ac0 + j + 1))
        up, whole, hi = k.bank[4 + j][:, 512 - n:512], k.act[:, j, 0:n], k.hid_hi[:, j, 0:n]
        dve.tensor_tensor(whole, whole, up, ALU.mult).then_inc(k.raw_ready.sem, 1)
        dve.wait_ge(k.raw_ready.sem, m + (self.hd0 + j + 1))
        if not isinstance(m, int) or m + j >= 2:
            dve.wait_ge(k.down_used.sem, m + (self.w0 + j - 1))
        dve.tensor_copy(hi, whole).then_inc(k.hid_hi_ready.sem, 1)
        dve.wait_ge(k.hid_hi_ready.sem, m + (self.hd0 + j + 1))
        dve.tensor_tensor(k.hid_lo[:, j, 0:n], whole, hi.bitcast(F32), ALU.subtract).then_inc(k.hid_ready.sem, 1)

    def vector(self, dve):
        k = self.k
        wait_all(dve, self.before)
        self._units(dve, in_lo, self._down_lo, self._multiply)
        dve.wait_ge(k.down_used.sem, self.w0 + self.units)
        for t in range(TT):
            for n in range(D // BLK):
                read_out(k, dve, k.bank[t * 2 + n][:], t, (n * BLK, (n + 1) * BLK), self.how).then_inc(k.acc_read_dve.sem, 1)


class Linear(Stage):

    def __init__(self, core, before, w, how, dst=None):
        super().__init__(core, before)
        self.w, self.how, self.dst = core.dram[w], how, dst
        n = self.w.shape[1]
        self.blocks = [(lo, min(lo + BLK, n)) for lo in range(0, n, BLK)]
        nb = len(self.blocks)
        self.u0 = core.in_units
        core.in_units += 2 * nb
        self.ar0 = core.acc_ready.plan(nb)
        self.ra0 = core.acc_read_act.plan(nb)
        self.rd0 = core.acc_read_dve.plan(nb)
        self.done = [(core.acc_read_act.sem, self.ra0 + nb), (core.acc_read_dve.sem, self.rd0 + nb)]

    def sync(self, sp):
        k = self.k
        for b, (lo, hi) in enumerate(self.blocks):
            for h in range(2):
                g = self.u0 + 2 * b + h
                s = g % RING
                if g >= RING:
                    sp.wait_ge(k.in_lo_ready.sem, g - RING + 1)
                sp.dma_start(k.ring_in[:, s, :].rearrange("p (c n) -> p c n", c=4)[:, :, 0:hi - lo],
                             self.w[h * BLK:(h + 1) * BLK, lo:hi].rearrange("(c p) n -> p c n", p=P)).then_inc(k.in_landed[s].sem, 16)

    def tensor(self, pe):
        k = self.k
        wait_all(pe, self.before)
        for b, (lo, hi) in enumerate(self.blocks):
            if b >= 2:
                pe.wait_ge(k.acc_read_act.sem, self.ra0 + b - 1)
                pe.wait_ge(k.acc_read_dve.sem, self.rd0 + b - 1)
            for h in range(2):
                g = self.u0 + 2 * b + h
                s = g % RING
                pe.wait_ge(k.in_lo_ready.sem, g + 1)
                w_hi = k.in_hi[:, s, :].rearrange("p (c n) -> p c n", c=4)[:, :, 0:hi - lo]
                w_lo = k.in_lo[:, s, :].rearrange("p (c n) -> p c n", c=4)[:, :, 0:hi - lo]
                for t in range(TT):
                    out = k.bank[(b % 2) * 2 + t][:, 0:hi - lo]
                    for c in range(4):
                        tok = slice(t * P, (t + 1) * P)
                        f_hi, f_lo = k.feat_hi[:, 4 * h + c, tok], k.feat_lo[:, 4 * h + c, tok]
                        pe.matmul(out, f_hi, w_hi[:, c, :], start=(h == 0 and c == 0), stop=False)
                        pe.matmul(out, f_hi, w_lo[:, c, :], start=False, stop=False)
                        last = pe.matmul(out, f_lo, w_hi[:, c, :], start=False, stop=(h == 1 and c == 3))
                last.then_inc(k.in_used.sem, 1)

    def _split(self, eng, split, b):
        if b + 1 < len(self.blocks):
            for h in range(2):
                split(self.k, eng, self.u0 + 2 * b + 2 + h)

    def _ready(self, eng, b):
        eng.wait_ge(self.k.in_used.sem, self.u0 + 2 * b + 2)

    def scalar(self, act):
        k = self.k
        wait_all(act, self.before)
        for b, (lo, hi) in enumerate(self.blocks):
            self._split(act, in_hi, b)
            self._ready(act, b)
            acc = k.bank[(b % 2) * 2][:, 0:hi - lo]
            if isinstance(self.how, str) and self.how in ("store", "y"):
                dst = self.dst if self.how == "store" else k.y
                act.copy(dst[:, 0, lo:hi], acc).then_inc(k.acc_read_act.sem, 1)
            else:
                act.copy(k.y[:, 0, lo:hi], acc).then_inc(k.acc_read_act.sem, 1)

    def vector(self, dve):
        k = self.k
        wait_all(dve, self.before)
        for b, (lo, hi) in enumerate(self.blocks):
            self._split(dve, in_lo, b)
            self._ready(dve, b)
            acc = k.bank[(b % 2) * 2 + 1][:, 0:hi - lo]
            if isinstance(self.how, str) and self.how in ("store", "y"):
                dst = self.dst if self.how == "store" else k.y
                dve.tensor_copy(dst[:, 1, lo:hi], acc).then_inc(k.acc_read_dve.sem, 1)
            else:
                k.dve_link(dve, read_out(k, dve, acc, 1, (lo, hi), self.how))
                dve.wait_ge(k.acc_read_act.sem, self.ra0 + b + 1)
                read_out(k, dve, k.y[:, 0, lo:hi], 0, (lo, hi), self.how).then_inc(k.acc_read_dve.sem, 1)


class Rope(Stage):

    def __init__(self, core, before, parts, at):
        super().__init__(core, before)
        self.parts = parts
        heads = sum(p[2] for p in parts)
        self.cosed = core.arena[:, at:at + TT * heads * HEAD].rearrange("p (t n d) -> p t n d", t=TT, d=HEAD)
        at += TT * heads * HEAD
        self.sined = core.arena[:, at:at + TT * heads * HEAD].rearrange("p (t n d) -> p t n d", t=TT, d=HEAD)
        self.n = TT * len(parts)
        self.sines = core.rope_sines.plan(2 * self.n)
        self.cosines = core.rope_cosines.plan(self.n)
        self.dsts = TT * sum(len(p[1]) for p in parts)
        self.r0 = core.rope_done.plan(self.dsts)
        self.done = [(core.rope_done.sem, self.r0 + self.dsts)]

    def _views(self):
        for t in range(TT):
            at = 0
            for view, dsts, heads in self.parts:
                yield t, at, view(t), dsts, heads
                at += heads

    def gpsimd(self, pool):
        k = self.k
        wait_all(pool, self.before)
        for t, at, q, _, heads in self._views():
            h = HEAD // 2
            out = self.sined[:, t, at:at + heads, :]
            for lo, other in ((0, h), (h, 0)):
                sin = k.c("sin", t * HEAD + lo, t * HEAD + lo + h).unsqueeze(1).broadcast_to([P, heads, h])
                pool.tensor_tensor(out[:, :, lo:lo + h], q[:, :, other:other + h], sin, ALU.mult).then_inc(k.rope_sines.sem, 1)

    def vector(self, dve):
        k = self.k
        wait_all(dve, self.before)
        for t, at, q, _, heads in self._views():
            cos = k.c("cos", t * HEAD, (t + 1) * HEAD).unsqueeze(1).broadcast_to([P, heads, HEAD])
            dve.tensor_tensor(self.cosed[:, t, at:at + heads, :], q, cos, ALU.mult).then_inc(k.rope_cosines.sem, 1)
        dve.wait_ge(k.rope_sines.sem, self.sines + 2 * self.n)
        dve.wait_ge(k.rope_cosines.sem, self.cosines + self.n)
        for t, at, q, dsts, heads in self._views():
            for dst in dsts:
                dve.tensor_tensor(dst(t), self.cosed[:, t, at:at + heads, :], self.sined[:, t, at:at + heads, :],
                                  ALU.add).then_inc(k.rope_done.sem, 1)


class Job:

    def __init__(self, q, k, v, gate=None):
        self.q, self.k, self.v, self.gate = q, k, v, gate


class Attention(Stage):

    def __init__(self, core, before, groups, mask, at, out, sinks=None, opener=None):
        super().__init__(core, before)
        k = core
        self.groups, self.mask, self.out, self.sinks, self.opener = groups, mask, out, sinks, opener
        self.jobs = [(g, slot, job) for g, (jobs) in enumerate(groups) for slot, job in jobs]
        n = self.n = len(self.jobs)
        wide = 384
        a = k.arena
        self.s = [a[:, at + i * wide:at + (i + 1) * wide] for i in range(2)]
        self.p = [a[:, at + (2 + i) * wide:at + (3 + i) * wide] for i in range(2)]
        self.pT = [a[:, at + (4 + i) * wide:at + (5 + i) * wide] for i in range(2)]
        at += 6 * wide
        self.stat = [a[:, at + 16 * i:at + 16 * (i + 1)] for i in range(2)]
        self.scored0, self.masked0 = k.att_scored.plan(n), k.att_masked.plan(2 * n)
        self.neg0, self.exp0 = k.att_negmax.plan(n), k.att_exp.plan(n)
        self.prob0, self.turn0 = k.att_probs.plan(n), k.att_turned.plan(n)
        self.read0, self.pv0 = k.att_read.plan(n), k.att_pv.plan(n)
        self.out0 = k.att_out.plan(len(groups))
        self.done = [(k.att_out.sem, self.out0 + len(groups))]

    def _scores(self, pe, j):
        k, job = self.k, self.jobs[j][2]
        if j >= 2:
            pe.wait_ge(k.att_masked.sem, self.masked0 + 2 * (j - 1))
        bank = k.bank[j % 2]
        pe.matmul(bank[:, 0:P], job.q(0), job.k(0, P), start=True, stop=True)
        pe.matmul(bank[:, P:3 * P], job.q(1), job.k(0, 2 * P), start=True, stop=True).then_inc(k.att_scored.sem, 1)

    def _turn(self, pe, j):
        k = self.k
        pe.wait_ge(k.att_probs.sem, self.prob0 + j + 1)
        if j >= 2:
            pe.wait_ge(k.att_read.sem, self.read0 + j - 1)
        for i in range(3):
            last = pe.transpose(k.bank[2 + j % 2][:, i * P:(i + 1) * P], self.p[j % 2][:, i * P:(i + 1) * P], k.c("ident"))
        last.then_inc(k.att_turned.sem, 1)

    def _values(self, pe, j):
        k = self.k
        g, slot, job = self.jobs[j]
        first = j == 0 or self.jobs[j - 1][0] != g
        final = j == self.n - 1 or self.jobs[j + 1][0] != g
        bank = k.bank[4 + g % 2]
        if first and g >= 2:
            pe.wait_ge(k.att_out.sem, self.out0 + g - 1)
        if first and self.opener:
            self.opener(pe, g, bank)
        pe.wait_ge(k.att_read.sem, self.read0 + j + 1)
        pT, lo = self.pT[j % 2], slot * HEAD
        start = first and not self.opener
        pe.matmul(bank[:, lo:lo + HEAD], pT[:, 0:P], job.v(0), start=start, stop=False, skip_group_check=True)
        pe.matmul(bank[:, 256 + lo:256 + lo + HEAD], pT[:, P:2 * P], job.v(0), start=False, stop=False, skip_group_check=True)
        pe.matmul(bank[:, 256 + lo:256 + lo + HEAD], pT[:, 2 * P:3 * P], job.v(1), start=False, stop=final,
                  skip_group_check=True).then_inc(k.att_pv.sem, 1)

    def tensor(self, pe):
        wait_all(pe, self.before)
        for j in range(self.n + 2):
            if j < self.n:
                self._scores(pe, j)
            if 1 <= j <= self.n:
                self._turn(pe, j - 1)
            if j >= 2:
                self._values(pe, j - 2)

    def _mask(self, dve, j):
        k, st = self.k, self.stat[j % 2]
        dve.wait_ge(k.att_scored.sem, self.scored0 + j + 1)
        if j >= 2:
            dve.wait_ge(k.att_exp.sem, self.exp0 + j - 1)
        for t, lo, hi in ((0, 0, P), (1, P, 3 * P)):
            dve.tensor_tensor_reduce(self.s[j % 2][:, lo:hi], k.bank[j % 2][:, lo:hi], k.c(self.mask, lo, hi),
                                     1.0, NEG, ALU.add, ALU.max, st[:, t:t + 1]).then_inc(k.att_masked.sem, 1)
        dve.wait_ge(k.att_masked.sem, self.masked0 + 2 * (j + 1))
        scale = HEAD ** -0.5
        if self.sinks is None:
            ins = dve.tensor_scalar(st[:, 2:4], st[:, 0:2], -scale, None, ALU.mult)
        else:
            ins = dve.tensor_scalar(st[:, 2:4], st[:, 0:2], -scale, self.sinks(j, True), ALU.mult, ALU.min)
        ins.then_inc(k.att_negmax.sem, 1)

    def _probs(self, dve, j):
        k, st, job = self.k, self.stat[j % 2], self.jobs[j][2]
        dve.wait_ge(k.att_exp.sem, self.exp0 + j + 1)
        if self.sinks is not None:
            k.dve_link(dve, dve.tensor_tensor(st[:, 4:6], st[:, 4:6], st[:, 10:12], ALU.add))
        k.dve_link(dve, dve.reciprocal(st[:, 6:8], st[:, 4:6]))
        if job.gate is not None:
            k.dve_link(dve, dve.tensor_tensor(st[:, 6:8], st[:, 6:8], job.gate, ALU.mult))
        p = self.p[j % 2]
        dve.tensor_scalar(p[:, 0:P], p[:, 0:P], st[:, 6:7], None, ALU.mult)
        dve.tensor_scalar(p[:, P:3 * P], p[:, P:3 * P], st[:, 7:8], None, ALU.mult).then_inc(k.att_probs.sem, 1)

    def vector(self, dve):
        k = self.k
        wait_all(dve, self.before)
        for j in range(self.n + 3):
            if j < self.n:
                self._mask(dve, j)
            if 1 <= j <= self.n:
                self._probs(dve, j - 1)
            if j >= 3 and (j - 3 == self.n - 1 or self.jobs[j - 3][0] != self.jobs[j - 2][0]):
                g = self.jobs[j - 3][0]
                dve.wait_ge(k.att_pv.sem, self.pv0 + j - 2)
                heads = len({slot for slot, _ in self.groups[g]})
                dve.tensor_copy(self.out[:, :, g * 256:g * 256 + heads * HEAD], k.bank_tiles(4 + g % 2)[:, :, 0:heads * HEAD]).then_inc(k.att_out.sem, 1)

    def scalar(self, act):
        k = self.k
        wait_all(act, self.before)
        scale = HEAD ** -0.5
        for j in range(self.n + 1):
            if j < self.n:
                st = self.stat[j % 2]
                act.wait_ge(k.att_negmax.sem, self.neg0 + j + 1)
                if j >= 2:
                    act.wait_ge(k.att_turned.sem, self.turn0 + j - 1)
                if self.sinks is not None:
                    for t in range(TT):
                        act.activation(st[:, 10 + t:11 + t], self.sinks(j, False), ACT.Exp, bias=st[:, 2 + t:3 + t])
                for t, lo, hi in ((0, 0, P), (1, P, 3 * P)):
                    last = act.activation(self.p[j % 2][:, lo:hi], self.s[j % 2][:, lo:hi], ACT.Exp,
                                          bias=st[:, 2 + t:3 + t], scale=scale, accum_out=st[:, 4 + t:5 + t])
                last.then_inc(k.att_exp.sem, 1)
            if j >= 1:
                i = j - 1
                act.wait_ge(k.att_turned.sem, self.turn0 + i + 1)
                if i >= 2:
                    act.wait_ge(k.att_pv.sem, self.pv0 + i - 1)
                act.copy(self.pT[i % 2][:], k.bank[2 + i % 2][:, 0:3 * P]).then_inc(k.att_read.sem, 1)


class StickBreaking(Stage):

    WIDE = 384

    def __init__(self, core, before, qT, kT, v, at, out):
        super().__init__(core, before)
        k, w = core, self.WIDE
        self.qT, self.kT, self.v, self.out = qT, kT, v, out
        a = k.arena
        self.e = [a[:, at + i * w:at + (i + 1) * w] for i in range(2)]
        self.sp = [a[:, at + (2 + i) * w:at + (3 + i) * w] for i in range(2)]
        self.w = [a[:, at + (4 + i) * w:at + (5 + i) * w] for i in range(2)]
        n = self.n = HEADS
        self.z0, self.ab0, self.sp0 = k.att_scored.plan(n), k.sb_logs.plan(n), k.sb_softplus.plan(n)
        self.sum0, self.mk0, self.w0 = k.sb_sums.plan(n), k.att_masked.plan(n), k.att_probs.plan(n)
        self.pv0, self.out0 = k.att_pv.plan(n), k.att_out.plan(n // 4)
        self.done = [(k.att_out.sem, self.out0 + n // 4)]

    @staticmethod
    def _diagonal(ap):
        return ap.rearrange("p (b n) -> p b n", n=P)[:, 0:3:2, :]

    def tensor(self, pe):
        k = self.k
        wait_all(pe, self.before)
        for j in range(self.n + 2):
            if j < self.n:
                if j >= 2:
                    pe.wait_ge(k.att_probs.sem, self.w0 + j - 1)
                bank = k.bank[j % 3]
                pe.matmul(bank[:, 0:256], self.kT(j)[:, 0:P], self.qT(j), start=True, stop=False, skip_group_check=True)
                pe.matmul(bank[:, 256:384], self.kT(j)[:, P:256], self.qT(j)[:, P:256], start=False, stop=False,
                          skip_group_check=True).then_inc(k.att_scored.sem, 1)
            if 1 <= j <= self.n:
                i = j - 1
                bank, sp = k.bank[i % 3], self.sp[i % 2]
                pe.wait_ge(k.sb_softplus.sem, self.sp0 + i + 1)
                pe.matmul(bank[:, 0:256], k.c("minus_tri"), sp[:, 0:256], start=False, stop=False, skip_group_check=True)
                pe.matmul(bank[:, P:256], k.c("minus_ones"), sp[:, 256:384], start=False, stop=False, skip_group_check=True)
                pe.matmul(bank[:, 256:384], k.c("minus_tri"), sp[:, 256:384], start=False, stop=True,
                          skip_group_check=True).then_inc(k.sb_sums.sem, 1)
            if j >= 2:
                i = j - 2
                g, lo = i // 4, (i % 4) * HEAD
                bank, w = k.bank[4 + g % 2], self.w[i % 2]
                if i % 4 == 0 and g >= 2:
                    pe.wait_ge(k.att_out.sem, self.out0 + g - 1)
                pe.wait_ge(k.att_probs.sem, self.w0 + i + 1)
                pe.matmul(bank[:, lo:lo + HEAD], w[:, 0:P], self.v(i, 0), start=i % 4 == 0, stop=False, skip_group_check=True)
                pe.matmul(bank[:, 256 + lo:256 + lo + HEAD], w[:, P:256], self.v(i, 0), start=False, stop=False, skip_group_check=True)
                pe.matmul(bank[:, 256 + lo:256 + lo + HEAD], w[:, 256:384], self.v(i, 1), start=False, stop=i % 4 == 3,
                          skip_group_check=True).then_inc(k.att_pv.sem, 1)

    def scalar(self, act):
        k = self.k
        wait_all(act, self.before)
        act.preload_act_table_set("natural_log_exp_and_others")
        for j in range(self.n + 1):
            if j < self.n:
                e = self.e[j % 2]
                act.wait_ge(k.att_scored.sem, self.z0 + j + 1)
                if j >= 2:
                    act.wait_ge(k.sb_softplus.sem, self.sp0 + j - 1)
                k.act_link(act, act.activation(e, k.bank[j % 3][:, 0:384], ACT.Abs))
                k.act_link(act, act.activation(e, e, ACT.Exp, scale=-1.0))
                act.activation(e, e, ACT.Ln, bias=1.0).then_inc(k.sb_logs.sem, 1)
            if j >= 1:
                i = j - 1
                act.wait_ge(k.att_masked.sem, self.mk0 + i + 1)
                if i >= 2:
                    act.wait_ge(k.att_pv.sem, self.pv0 + i - 1)
                act.activation(self.w[i % 2], k.bank[i % 3][:, 0:384], ACT.Exp).then_inc(k.att_probs.sem, 1)

    def vector(self, dve):
        k = self.k
        wait_all(dve, self.before)
        for j in range(self.n + 3):
            if j < self.n:
                sp = self.sp[j % 2]
                dve.wait_ge(k.sb_logs.sem, self.ab0 + j + 1)
                if j >= 2:
                    dve.wait_ge(k.sb_sums.sem, self.sum0 + j - 1)
                k.dve_link(dve, dve.scalar_tensor_tensor(sp, k.bank[j % 3][:, 0:384], 0.0, self.e[j % 2], ALU.max, ALU.add))
                d = self._diagonal(sp)
                dve.tensor_tensor(d, d, k.c("before01").unsqueeze(1).broadcast_to([P, 2, P]), ALU.mult).then_inc(k.sb_softplus.sem, 1)
            if 1 <= j <= self.n:
                i = j - 1
                dve.wait_ge(k.sb_sums.sem, self.sum0 + i + 1)
                d = self._diagonal(k.bank[i % 3][:, 0:384])
                dve.tensor_tensor(d, d, k.c("beforeadd").unsqueeze(1).broadcast_to([P, 2, P]), ALU.add).then_inc(k.att_masked.sem, 1)
            if j >= 3 and (j - 3) % 4 == 3:
                g = (j - 3) // 4
                dve.wait_ge(k.att_pv.sem, self.pv0 + 4 * (g + 1))
                dve.tensor_copy(self.out[:, :, g * 256:(g + 1) * 256], k.bank_tiles(4 + g % 2)).then_inc(k.att_out.sem, 1)


class ShortConv(Stage):

    def __init__(self, core, before, bT, hT, at):
        super().__init__(core, before)
        self.bT, self.hT = bT, hT
        self.acc = core.arena[:, at:at + KC * TOKENS].rearrange("p (c n) -> p c n", c=KC)
        self.d0 = core.conv_done.plan(1)
        self.done = [(core.conv_done.sem, self.d0 + 1)]

    def vector(self, dve):
        k, n = self.k, TOKENS
        wait_all(dve, self.before)
        for c in range(KC):
            last = dve.tensor_scalar(self.acc[:, c, :], self.hT[:, c, :], k.col("conv_w_3_2", c), None, ALU.mult)
        k.dve_link(dve, last)
        for tap, back in ((1, 1), (0, 2)):
            for c in range(KC):
                acc = self.acc[:, c, back:n]
                last = dve.scalar_tensor_tensor(acc, self.hT[:, c, 0:n - back], k.col(f"conv_w_3_{tap}", c), acc, ALU.mult, ALU.add)
            k.dve_link(dve, last)
        k.dve_link(dve, dve.tensor_tensor(self.acc[:], self.acc[:], self.bT, ALU.mult))
        feat_from(k, dve, self.acc[:], 0, KC).then_inc(k.conv_done.sem, 1)


class Product(Stage):

    def __init__(self, core, before, out, a, b, silu=False):
        super().__init__(core, before)
        self.out, self.a, self.b, self.silu = out, a, b, silu
        self.s0 = core.silu_ready.plan(TT if silu else 0)
        self.d0 = core.product_done.plan(TT)
        self.done = [(core.product_done.sem, self.d0 + TT)]

    def scalar(self, act):
        if self.silu:
            wait_all(act, self.before)
            for t in range(TT):
                act.activation(self.a(t), self.a(t), ACT.Silu).then_inc(self.k.silu_ready.sem, 1)

    def vector(self, dve):
        wait_all(dve, self.before)
        for t in range(TT):
            if self.silu:
                dve.wait_ge(self.k.silu_ready.sem, self.s0 + t + 1)
            dve.tensor_tensor(self.out(t), self.a(t), self.b(t), ALU.mult).then_inc(self.k.product_done.sem, 1)


def heads_view(k, at, chunks):
    return k.arena[:, at:at + chunks * TOKENS].rearrange("p (c n) -> p c n", c=chunks)


def o_to_x(core, before, w_out, how):
    turn = FeatTurn(core, before, lambda t, c: core.y[:, t, c * P:(c + 1) * P])
    return [turn, Linear(core, turn, w_out, how)]


def stick_breaking(core, before, w_qkv, w_o):
    k = core
    proj = Linear(k, before, w_qkv, "store", dst=k.proj)
    early = Presplit(k, proj)
    qk = heads_view(k, 0, 16)
    turn = Turn(k, proj, lambda t, c: k.proj[:, t, c * P:(c + 1) * P], qk, 16,
                scale=lambda c: HEAD ** -0.5 if c < KC else 1.0)
    rows = lambda h: slice((h % 2) * HEAD, (h % 2 + 1) * HEAD)
    att = StickBreaking(k, turn, lambda h: qk[rows(h), h // 2, :], lambda h: qk[rows(h), KC + h // 2, :],
                        lambda h, t: k.proj[:, t, 2 * D + h * HEAD:2 * D + (h + 1) * HEAD], 16 * TOKENS, k.y)
    return [proj, early, turn, att] + o_to_x(k, att, w_o, "y")


def short_conv(core, before):
    k = core
    proj = Linear(k, before, "conv_w_in_3", "store", dst=k.proj)
    early = Presplit(k, proj)
    prod = Product(k, proj, lambda t: k.y[:, t, :], lambda t: k.proj[:, t, D:2 * D], lambda t: k.proj[:, t, 2 * D:3 * D])
    bh = heads_view(k, 0, 16)
    turn = Turn(k, prod, lambda t, c: k.proj[:, t, c * P:(c + 1) * P] if c < KC else k.y[:, t, (c - KC) * P:(c - KC + 1) * P], bh, 16)
    conv = ShortConv(k, turn, bh[:, 0:KC, :], bh[:, KC:16, :], 16 * TOKENS)
    return [proj, early, prod, turn, conv, Linear(k, conv, "conv_w_out_3", "y")]


def swa(core, before):
    k = core
    proj = Linear(k, before, "swa_w_in", "store", dst=k.proj)
    early = Presplit(k, proj)
    sinks = Sinks(k, proj, 18000)
    kd = k.arena[:, 10000:10000 + 512].rearrange("p (t g two d) -> p t g two d", t=TT, g=2, two=2)
    view = lambda lo, n: (lambda t: k.proj[:, t, lo:lo + n * HEAD].rearrange("p (n d) -> p n d", d=HEAD))
    rope = Rope(k, sinks, [(view(0, 16), [view(0, 16)], 16),
                           (view(D, 2), [lambda t: kd[:, t, :, 0, :], lambda t: kd[:, t, :, 1, :]], 2)], 11000)
    qk = heads_view(k, 0, 10)
    turn = Turn(k, rope, lambda t, c: k.proj[:, t, c * P:(c + 1) * P] if c < KC
                else kd[:, t, c - KC, :, :].rearrange("p two d -> p (two d)"), qk, 10)
    rows = lambda h: slice((h % 2) * HEAD, (h % 2 + 1) * HEAD)

    def job(h):
        g = h // 8
        return Job(lambda t: qk[rows(h), h // 2, t * P:(t + 1) * P], lambda lo, hi: qk[rows(h), KC + g, lo:hi],
                   lambda t: k.proj[:, t, D + 128 + g * HEAD:D + 128 + (g + 1) * HEAD])
    att = Attention(k, turn, [[(s, job(4 * g + s)) for s in range(4)] for g in range(4)], "window", 2560, k.y,
                    sinks=lambda j, neg: sinks.minus(j) if neg else sinks.plain(j))
    return [proj, early, sinks, rope, turn, att] + o_to_x(k, att, "swa_w_out", "add")


class Sinks(Stage):

    def __init__(self, core, before, at):
        super().__init__(core, before)
        self.s = core.arena[:, at:at + 32]
        self.l0 = core.row_landed.plan(16)
        self.n0 = core.sinks_ready.plan(1)
        self.done = self.before + [(core.sinks_ready.sem, self.n0 + 1)]

    def plain(self, h):
        return self.s[:, h:h + 1]

    def minus(self, h):
        return self.s[:, 16 + h:17 + h]

    def gpsimd(self, pool):
        k = self.k
        wait_all(pool, self.before)
        pool.dma_start(self.s[:, 0:16], k.dram["swa_sinks"][0:1, :].partition_broadcast(P)).then_inc(k.row_landed.sem, 16)
        pool.wait_ge(k.row_landed.sem, self.l0 + 16)
        pool.tensor_scalar(self.s[:, 16:32], self.s[:, 0:16], -1.0, None, ALU.mult).then_inc(k.sinks_ready.sem, 1)


def more_signals(k):
    k.rope_sines = k.sig("rope_sines")
    k.rope_cosines = k.sig("rope_cosines")
    k.rope_done = k.sig("rope_done")
    k.att_scored = k.sig("att_scored")
    k.att_masked = k.sig("att_masked")
    k.att_negmax = k.sig("att_negmax")
    k.att_exp = k.sig("att_exp")
    k.att_probs = k.sig("att_probs")
    k.att_turned = k.sig("att_turned")
    k.att_read = k.sig("att_read")
    k.att_pv = k.sig("att_pv")
    k.att_out = k.sig("att_out")
    k.sb_logs = k.sig("sb_logs")
    k.sb_softplus = k.sig("sb_softplus")
    k.sb_sums = k.sig("sb_sums")
    k.gate_exp = k.sig("gate_exp")
    k.gates_ready = k.sig("gates_ready")
    k.copies_done = k.sig("copies_done")
    k.cmp_w_landed = k.sig("cmp_w_landed")
    k.cmp_pairs = k.sig("cmp_pairs")
    k.cmp_zeroed = k.sig("cmp_zeroed")
    k.cmp_hidden = k.sig("cmp_hidden")
    k.cmp_gelu = k.sig("cmp_gelu")
    k.cmp_act = k.sig("cmp_act")
    k.cmp_keys = k.sig("cmp_keys")
    k.cmp_keys_read = k.sig("cmp_keys_read")
    k.cmp_scored = k.sig("cmp_scored")
    k.cmp_probs_in = k.sig("cmp_probs_in")
    k.cmp_probs = k.sig("cmp_probs")
    k.cmp_turned = k.sig("cmp_turned")
    k.cmp_turned_read = k.sig("cmp_turned_read")
    k.gate_spread = k.sig("gate_spread")
    k.gate_row = k.sig("gate_row")
    k.conv_done = k.sig("conv_done")
    k.silu_ready = k.sig("silu_ready")
    k.product_done = k.sig("product_done")
    k.sinks_ready = k.sig("sinks_ready")


class Gates(Stage):

    def __init__(self, core, before, at):
        super().__init__(core, before)
        self.g = core.arena[:, at:at + TT * 48].rearrange("p (t n) -> p t n", t=TT)
        self.e0 = core.gate_exp.plan(1)
        self.d0 = core.gates_ready.plan(1)
        self.done = self.before + [(core.gates_ready.sem, self.d0 + 1)]

    def scalar(self, act):
        wait_all(act, self.before)
        act.activation(self.g[:], self.k.proj[:, :, 2560:2608], ACT.Exp, scale=-1.0).then_inc(self.k.gate_exp.sem, 1)

    def vector(self, dve):
        k = self.k
        dve.wait_ge(k.gate_exp.sem, self.e0 + 1)
        k.dve_link(dve, dve.tensor_scalar(self.g[:], self.g[:], 1.0, None, ALU.add))
        dve.reciprocal(self.g[:], self.g[:]).then_inc(k.gates_ready.sem, 1)


class Compress(Stage):

    def __init__(self, core, before, q, kT, vT, gates, at):
        super().__init__(core, before)
        k = core
        self.q, self.kT, self.vT, self.gates = q, kT, vT, gates
        a = k.arena
        n = CMP_N

        def take(size):
            nonlocal at
            at += size
            return a[:, at - size:at]

        self.w1 = [take(2048).rearrange("p (l h) -> p l h", h=P) for _ in range(2)]
        self.w2 = [take(2 * HEAD) for _ in range(2)]
        self.pair = [take(4 * TOKENS).rearrange("p (g n) -> p g n", g=4) for _ in range(2)]
        self.hid = [take(8 * n) for _ in range(4)]
        self.bias = take(2)
        self.kcT = take(4 * n)
        self.values = take(4 * 256).rearrange("p (g n) -> p g n", g=4)
        self.probs = take(TT * HEADS * 32).rearrange("p (t h n) -> p t h n", t=TT, h=HEADS)
        self.s = take(TT * HEADS * n)
        self.stat = take(4 * TT * HEADS).rearrange("p (i n) -> p i n", i=4)
        self.turned = self.w1[0].rearrange("p l h -> p (l h)")[:, 0:8 * P].rearrange("p (t g n) -> p t g n", t=TT, g=4)
        self.w_landed0 = k.cmp_w_landed.plan(16 * 6)
        self.pair0 = k.cmp_pairs.plan(4)
        self.zero0 = k.cmp_zeroed.plan(2)
        self.hid0 = k.cmp_hidden.plan(1)
        self.gelu0 = k.cmp_gelu.plan(2)
        self.act0 = k.cmp_act.plan(2)
        self.kc0 = k.cmp_keys.plan(1)
        self.kr0 = k.cmp_keys_read.plan(1)
        self.sc0 = k.cmp_scored.plan(1)
        self.pi0 = k.cmp_probs_in.plan(1)
        self.pr0 = k.cmp_probs.plan(1)
        self.tu0 = k.cmp_turned.plan(2)
        self.tr0 = k.cmp_turned_read.plan(2)
        self.done = [(k.cmp_turned_read.sem, self.tr0 + 2)]

    def gpsimd(self, pool):
        k = self.k
        wait_all(pool, self.before)
        s = k.cmp_w_landed.sem
        for i, name in enumerate(("nsa_ck", "nsa_cv")):
            pool.dma_start(self.w1[i], k.dram[name + "_w1"].rearrange("(l p) h -> p l h", p=P)).then_inc(s, 16)
            for h in range(2):
                pool.dma_start(self.w2[i][:, h * HEAD:(h + 1) * HEAD], k.dram[name + "_w2"]).then_inc(s, 16)
        pool.memset(self.values[:], 0.0).then_inc(k.cmp_zeroed.sem, 1)
        pool.memset(self.probs[:], 0.0).then_inc(k.cmp_zeroed.sem, 1)

    def tensor(self, pe):
        k, n = self.k, CMP_N
        wait_all(pe, self.before)
        pe.wait_ge(k.cmp_w_landed.sem, self.w_landed0 + 96)
        pe.wait_ge(k.cmp_pairs.sem, self.pair0 + 4)
        for i in range(2):
            for l in range(CMP_LEN // 2):
                rhs = self.pair[i][:, :, 2 * l:2 * l + CMP_STRIDE * (n - 1) + 1:CMP_STRIDE]
                pe.matmul(k.bank[i][:, 0:4 * n], self.w1[i][:, l, :], rhs, start=l == 0, stop=l == 15)
                last = pe.matmul(k.bank[2 + i][:, 0:1], self.w1[i][:, l, :], k.col(("ck_pe", "cv_pe")[i], l), start=l == 0, stop=l == 15)
        last.then_inc(k.cmp_hidden.sem, 1)
        pe.wait_ge(k.cmp_gelu.sem, self.gelu0 + 2)
        hid = self.hid[3]
        pe.matmul(k.bank[0][:, 0:4 * n], self.w2[0], hid[:, 0:4 * n], start=True, stop=True)
        for g in range(4):
            for h in range(4):
                last = pe.matmul(k.bank[1][32 * h:32 * h + n, g * HEAD:(g + 1) * HEAD], hid[:, (4 + g) * n:(5 + g) * n],
                                 self.w2[1][:, 0:HEAD], start=True, stop=True)
        last.then_inc(k.cmp_keys.sem, 1)
        pe.wait_ge(k.cmp_keys_read.sem, self.kr0 + 1)
        for t in range(TT):
            for h in range(HEADS):
                g, rows = h // 4, slice((h % 2) * HEAD, (h % 2 + 1) * HEAD)
                lo = (t * (HEADS // 2) + h // 2) * n
                last = pe.matmul(k.bank[4 + h % 2][:, lo:lo + n], self.q(h)[:, t * P:(t + 1) * P], self.kcT[rows, g * n:(g + 1) * n],
                                 start=True, stop=True)
        last.then_inc(k.cmp_scored.sem, 1)
        pe.wait_ge(k.cmp_probs.sem, self.pr0 + 1)
        for t in range(TT):
            for g in range(4):
                last = pe.transpose(k.bank[2 + t][:, g * P:(g + 1) * P],
                                    self.probs[:, t, 4 * g:4 * g + 4, :].rearrange("p h n -> p (h n)"), k.c("ident"))
            last.then_inc(k.cmp_turned.sem, 1)

    def scalar(self, act):
        k = self.k
        wait_all(act, self.before)
        act.wait_ge(k.cmp_gelu.sem, self.gelu0 + 1)
        act.activation(self.hid[2], self.hid[1], ACT.Exp, scale=-2.0 * float(np.sqrt(2.0 / np.pi))).then_inc(k.cmp_act.sem, 1)
        act.wait_ge(k.cmp_probs_in.sem, self.pi0 + 1)
        act.activation(self.s, self.s, ACT.Exp).then_inc(k.cmp_act.sem, 1)

    def vector(self, dve):
        k, n = self.k, CMP_N
        wait_all(dve, self.before)
        for i, src in enumerate((self.kT, self.vT)):
            dve.tensor_copy(self.pair[i][0:64], src[0:64]).then_inc(k.cmp_pairs.sem, 1)
            dve.tensor_copy(self.pair[i][64:128, :, 0:TOKENS - 1], src[64:128, :, 1:TOKENS]).then_inc(k.cmp_pairs.sem, 1)
        link = lambda ins: k.dve_link(dve, ins)
        x, u, e, out = self.hid
        dve.wait_ge(k.cmp_hidden.sem, self.hid0 + 1)
        for i in range(2):
            link(dve.tensor_copy(self.bias[:, i:i + 1], k.bank[2 + i][:, 0:1]))
        for i in range(2):
            link(dve.tensor_scalar(x[:, i * 4 * n:(i + 1) * 4 * n], k.bank[i][:, 0:4 * n], self.bias[:, i:i + 1], None, ALU.add))
        link(dve.tensor_tensor(u, x, x, ALU.mult))
        link(dve.tensor_scalar(u, u, 0.044715, 1.0, ALU.mult, ALU.add))
        dve.tensor_tensor(u, u, x, ALU.mult).then_inc(k.cmp_gelu.sem, 1)
        dve.wait_ge(k.cmp_act.sem, self.act0 + 1)
        link(dve.tensor_scalar(e, e, 1.0, None, ALU.add))
        link(dve.reciprocal(e, e))
        dve.tensor_tensor(out, e, x, ALU.mult).then_inc(k.cmp_gelu.sem, 1)
        dve.wait_ge(k.cmp_keys.sem, self.kc0 + 1)
        dve.wait_ge(k.cmp_zeroed.sem, self.zero0 + 2)
        dve.tensor_copy(self.kcT, k.bank[0][:, 0:4 * n])
        for h in range(4):
            r = slice(32 * h, 32 * h + n)
            last = dve.tensor_copy(self.values[r, :, h * HEAD:(h + 1) * HEAD], k.bank[1][r, 0:256].rearrange("p (g d) -> p g d", g=4))
        last.then_inc(k.cmp_keys_read.sem, 1)
        rows = TT * HEADS
        s3 = self.s.rearrange("p (r n) -> p r n", n=n)
        wide = lambda i: self.stat[:, i, :].unsqueeze(2).broadcast_to([P, rows, n])
        dve.wait_ge(k.cmp_scored.sem, self.sc0 + 1)
        half = HEADS // 2 * n
        for t in range(TT):
            for odd in range(2):
                mask = k.c("cmpadd", t * n, (t + 1) * n).unsqueeze(1).broadcast_to([P, HEADS // 2, n])
                src = k.bank[4 + odd][:, t * half:(t + 1) * half].rearrange("p (h n) -> p h n", n=n)
                ins = dve.scalar_tensor_tensor(s3[:, t * HEADS + odd:(t + 1) * HEADS:2, :], src, HEAD ** -0.5, mask, ALU.mult, ALU.add)
        link(ins)
        link(dve.tensor_reduce(self.stat[:, 0, :], s3, AX.X, ALU.max))
        dve.tensor_tensor(s3, s3, wide(0), ALU.subtract).then_inc(k.cmp_probs_in.sem, 1)
        dve.wait_ge(k.cmp_act.sem, self.act0 + 2)
        link(dve.tensor_reduce(self.stat[:, 1, :], s3, AX.X, ALU.add))
        link(dve.reciprocal(self.stat[:, 2, :], self.stat[:, 1, :]))
        link(dve.tensor_tensor(self.stat[:, 3, :].rearrange("p (t h) -> p t h", t=TT), self.stat[:, 2, :].rearrange("p (t h) -> p t h", t=TT),
                               self.gates[:, :, 0:HEADS], ALU.mult))
        for t in range(TT):
            ok = k.c("cmp01", t * n, (t + 1) * n).unsqueeze(1).broadcast_to([P, HEADS, n])
            v = s3[:, t * HEADS:(t + 1) * HEADS, :]
            ins = dve.tensor_tensor(v, v, ok, ALU.mult)
        link(ins)
        for t in range(TT):
            v = s3[:, t * HEADS:(t + 1) * HEADS, :]
            w = self.stat[:, 3, t * HEADS:(t + 1) * HEADS].unsqueeze(2).broadcast_to([P, HEADS, n])
            last = dve.tensor_tensor(self.probs[:, t, :, 0:n], v, w, ALU.mult)
        last.then_inc(k.cmp_probs.sem, 1)
        for t in range(TT):
            dve.wait_ge(k.cmp_turned.sem, self.tu0 + t + 1)
            dve.tensor_copy(self.turned[:, t, :, :], k.bank[2 + t][:, :].rearrange("p (g n) -> p g n", g=4)).then_inc(k.cmp_turned_read.sem, 1)

    def opener(self, pe, g, bank):
        for t in range(TT):
            pe.matmul(bank[:, t * 256:(t + 1) * 256], self.turned[:, t, g, :], self.values[:, g, :],
                      start=t == 0, stop=False, skip_group_check=True)


def nsa(core, before):
    k = core
    proj = Linear(k, before, "nsa_w_in", "store", dst=k.proj)
    early = Presplit(k, proj)
    gates = Gates(k, proj, ARENA - 96)
    kd = k.arena[:, 6144:6144 + 4096].rearrange("p (t n two d) -> p t n two d", t=TT, n=16, two=2)
    q = lambda t: k.proj[:, t, 0:D].rearrange("p (n d) -> p n d", d=HEAD)
    kv = lambda b, i: (lambda t: k.proj[:, t, D + (2 * b + i) * 256:D + (2 * b + i + 1) * 256].rearrange("p (n d) -> p n d", d=HEAD))
    parts = [(q, [q], 16)]
    for b in range(3):
        parts.append((kv(b, 0), [(lambda t, b=b, i=i: kd[:, t, 4 * b:4 * b + 4, i, :]) for i in range(2)], 4))
    rope = Rope(k, gates, parts, 6144 + 4096)
    twice = Twice(k, rope, kv(0, 1), lambda t, i: kd[:, t, 12:16, i, :])
    T = heads_view(k, 0, 24)
    turn = Turn(k, twice, lambda t, c: k.proj[:, t, c * P:(c + 1) * P] if c < KC
                else kd[:, t, c - KC, :, :].rearrange("p two d -> p (two d)"), T, 24)
    rows = lambda h: slice((h % 2) * HEAD, (h % 2 + 1) * HEAD)
    cmp = Compress(k, turn, lambda h: T[rows(h), h // 2, :], T[:, KC:KC + 4, :], T[:, 20:24, :], gates.g, 6144)
    at = 6144 + 4096 + 256 + 2048 + 480 + 2 + 60 + 1024 + 1024 + 480 + 128

    def job(h, b):
        g = h // 4
        v = kv(b, 1)
        return Job(lambda t: T[rows(h), h // 2, t * P:(t + 1) * P], lambda lo, hi: T[rows(h), KC + 4 * b + g, lo:hi],
                   lambda t: v(t)[:, g, :], gate=gates.g[:, :, b * 16 + h])
    groups = [[(s, job(4 * g + s, b)) for s in range(4) for b in (1, 2)] for g in range(4)]
    att = Attention(k, cmp, groups, "causal", at, k.y, opener=cmp.opener)
    return [proj, early, gates, rope, twice, turn, cmp, att] + o_to_x(k, att, "nsa_w_out", "add")


class Twice(Stage):

    def __init__(self, core, before, src, dst):
        super().__init__(core, before)
        self.src, self.dst = src, dst
        self.d0 = core.copies_done.plan(4)
        self.done = self.before + [(core.copies_done.sem, self.d0 + 4)]

    def scalar(self, act):
        wait_all(act, self.before)
        for t in range(TT):
            for i in range(2):
                act.copy(self.dst(t, i), self.src(t)).then_inc(self.k.copies_done.sem, 1)


class Modulation:

    def __init__(self, core):
        k = self.k = core
        self.sum, self.w = k.mod_sum, k.mod_w
        self.columns = k.sb("mod_columns", 9, KC)
        self.gate_rows = k.sb("mod_gates", D)
        self.landed = [k.sig(f"mod_w_landed{i}") for i in range(2)]
        self.used = k.sig("mod_w_used")
        self.step = k.sig("mod_step")
        self.summed = k.sig("mod_summed")
        self.spread = k.sig("mod_spread")
        self.kept = k.sig("mod_kept")
        self.loads = 0

    def scale(self, branch):
        return lambda c: self.columns[:, 3 * branch + 1, c:c + 1]

    def shift(self, branch):
        return lambda c: self.columns[:, 3 * branch, c:c + 1]


class ModPart(Stage):

    def __init__(self, core, before, mod, branch):
        super().__init__(core, before)
        self.mod, self.branch = mod, branch
        self.l0 = mod.loads
        mod.loads += 27
        self.s0 = mod.summed.plan(1)

    def _load(self, pool, i):
        k, mod = self.k, self.mod
        g = self.l0 + i
        s = g % 2
        if g >= 2:
            pool.wait_ge(mod.used.sem, g - 1)
        v, c = 3 * self.branch + i // 9, i % 9
        if c < KC:
            pool.dma_start(mod.w[:, s, :], k.dram["w_ada_2"][c * P:(c + 1) * P, v * D:(v + 1) * D]).then_inc(mod.landed[s].sem, 16)
        else:
            pool.dma_start(mod.w[0:1, s, :], k.dram["b_ada_2"][0:1, v * D:(v + 1) * D]).then_inc(mod.landed[s].sem, 16)

    def gpsimd(self, pool):
        k, mod = self.k, self.mod
        wait_all(pool, self.before)
        if self.branch:
            pool.wait_ge(mod.kept.sem, 3 * self.branch)
        self._load(pool, 0)
        for i in range(27):
            if i + 1 < 27:
                self._load(pool, i + 1)
            g = self.l0 + i
            s, c, total = g % 2, i % 9, mod.sum[:, i // 9, :]
            pool.wait_ge(mod.landed[s].sem, 16 * (g // 2 + 1))
            if c == 0:
                pool.tensor_scalar(total, mod.w[:, s, :], k.col("c_2", c), 0.0, ALU.mult, ALU.add).then_inc(mod.used.sem, 1)
            elif c < KC:
                k.pool_link(pool, pool.tensor_scalar(mod.w[:, s, :], mod.w[:, s, :], k.col("c_2", c), 0.0, ALU.mult, ALU.add))
                pool.wait_ge(mod.used.sem, g)
                pool.tensor_tensor(total, total, mod.w[:, s, :], ALU.add).then_inc(mod.used.sem, 1)
            else:
                pool.wait_ge(mod.used.sem, g)
                pool.tensor_tensor(total[0:1], total[0:1], mod.w[0:1, s, :], ALU.add).then_inc(mod.used.sem, 1)
        pool.wait_ge(mod.used.sem, self.l0 + 27)
        pool.memset(mod.w[0:1, 0, 0:1], 0.0).then_inc(mod.summed.sem, 1)


class ModSpread(Stage):

    def __init__(self, core, before, mod, branch, gain):
        super().__init__(core, before)
        self.mod, self.branch, self.gain = mod, branch, gain
        self.p0 = mod.spread.plan(1)
        self.k0 = mod.kept.plan(3)
        self.done = self.before + [(mod.kept.sem, self.k0 + 3)]

    def tensor(self, pe):
        k, mod = self.k, self.mod
        wait_all(pe, self.before)
        pe.wait_ge(mod.summed.sem, self.branch + 1)
        one = k.c("ones", 0, 1)
        for i in range(2):
            for c in range(KC):
                pe.matmul(k.bank[0][:, i * KC + c:i * KC + c + 1], mod.sum[:, i, c * P:(c + 1) * P], one, start=True, stop=True)
        r = 32 * self.branch
        for n in range(2):
            last = pe.matmul(k.bank[1 + n][r:r + 1, :], one, mod.sum[:, 2, n * BLK:(n + 1) * BLK], start=True, stop=True)
        last.then_inc(mod.spread.sem, 1)

    def vector(self, dve):
        k, mod, b = self.k, self.mod, self.branch
        wait_all(dve, self.before)
        dve.wait_ge(mod.spread.sem, b + 1)
        dve.tensor_copy(mod.columns[:, 3 * b, :], k.bank[0][:, 0:KC])
        dve.scalar_tensor_tensor(mod.columns[:, 3 * b + 1, :], k.bank[0][:, KC:2 * KC], 1.0, k.col(self.gain, 0, KC),
                                 ALU.add, ALU.mult).then_inc(mod.kept.sem, 1)
        r = slice(32 * b, 32 * b + 1)
        half = 1.0 if b == 1 else 0.5
        for n in range(2):
            dve.tensor_scalar(mod.gate_rows[r, n * BLK:(n + 1) * BLK], k.bank[1 + n][r, :], 1.0, half, ALU.add, ALU.mult).then_inc(mod.kept.sem, 1)


class GateRow(Stage):

    def __init__(self, core, before, mod, branch):
        super().__init__(core, before)
        self.mod, self.branch = mod, branch
        self.p0 = core.gate_spread.plan(1)
        self.d0 = core.gate_row.plan(1)
        self.done = self.before + [(core.gate_row.sem, self.d0 + 1)]

    def tensor(self, pe):
        k, r = self.k, 32 * self.branch
        wait_all(pe, self.before)
        for n in range(2):
            last = pe.matmul(k.bank[n][:], k.c("ones", 0, P)[r:r + 1, :], self.mod.gate_rows[r:r + 1, n * BLK:(n + 1) * BLK], start=True, stop=True)
        last.then_inc(k.gate_spread.sem, 1)

    def vector(self, dve):
        k = self.k
        wait_all(dve, self.before)
        dve.wait_ge(k.gate_spread.sem, self.p0 + 1)
        for n in range(2):
            last = dve.tensor_copy(k.row[:, n * BLK:(n + 1) * BLK], k.bank[n][:])
        last.then_inc(k.gate_row.sem, 1)


class Mlstm(Stage):

    def __init__(self, core, before, xT, at):
        super().__init__(core, before)
        k = core
        self.xT = xT
        a = k.arena

        def take(size):
            nonlocal at
            at += size
            return a[:, at - size:at]

        n = TOKENS
        self.w = [take(512).rearrange("p (h e) -> p h e", h=4) for _ in range(3)]
        self.w_if = take(96).rearrange("p (c n) -> p c n", n=8)
        self.b_if = take(2)
        self.conv = take(4 * n).rearrange("p (c n) -> p c n", c=4)
        self.qk = take(8 * n).rearrange("p (h i n) -> p h i n", h=4, i=2)
        self.vT = take(4 * n).rearrange("p (h n) -> p h n", h=4)
        self.v = take(TT * 4 * 129).rearrange("p (t h n) -> p t h n", t=TT, h=4)
        self.rows = take(8 * n).rearrange("p (i n) -> p i n", i=8)
        self.cols = take(16).rearrange("p (t i h) -> p t i h", t=TT, i=2)
        self.e = take(384)
        self.weights = take(384)
        self.stat = take(8 * 4).rearrange("p (i n) -> p i n", i=4)
        assert at <= ARENA
        self.w_landed = k.sig("m_w_landed").sem
        self.convolved = k.sig("m_convolved").sem
        self.silu = k.sig("m_silu").sem
        self.projected = k.sig("m_projected").sem
        self.read_act = k.sig("m_read_act").sem
        self.read_dve = k.sig("m_read_dve").sem
        self.gated = k.sig("m_gated").sem
        self.gate_in = k.sig("m_gate_in").sem
        self.gate_log = k.sig("m_gate_log").sem
        self.rows_ready = k.sig("m_rows_ready").sem
        self.cols_turned = k.sig("m_cols_turned").sem
        self.cols_read = k.sig("m_cols_read").sem
        self.scored = k.sig("m_scored").sem
        self.masked = k.sig("m_masked").sem
        self.exped = k.sig("m_exped").sem
        self.weighted = k.sig("m_weighted").sem
        self.summed = k.sig("m_summed").sem
        self.expm = k.sig("m_expm").sem
        self.normed = k.sig("m_normed").sem
        self.squares = k.sig("m_squares").sem
        self.rstd = k.sig("m_rstd").sem
        self.mean = k.sig("m_mean").sem
        self.done = [(self.normed, 1)]

    def gpsimd(self, pool):
        k = self.k
        wait_all(pool, self.before)
        for i, n in enumerate(("w_q_m_2", "w_k_m_2", "w_v_m_2")):
            pool.dma_start(self.w[i], k.dram[n].rearrange("h d e -> d h e")).then_inc(self.w_landed, 16)
        pool.dma_start(self.w_if, k.dram["w_if_2"].rearrange("(c p) n -> p c n", p=P)).then_inc(self.w_landed, 16)
        pool.dma_start(self.b_if[0:4, :], k.dram["b_if_2"]).then_inc(self.w_landed, 16)
        pool.wait_ge(self.squares, 1)
        k.pool_link(pool, pool.tensor_scalar(self.stat[:, 2, :], self.stat[:, 1, :], 1.0 / P, EPS, ALU.mult, ALU.add))
        pool.tensor_tensor(self.stat[:, 3, :], self.stat[:, 2, :], k.minus_half[:, 0:8], ALU.pow).then_inc(self.rstd, 1)

    def tensor(self, pe):
        k, n = self.k, TOKENS
        wait_all(pe, self.before)
        pe.wait_ge(self.w_landed, 80)
        pe.wait_ge(self.silu, 1)
        for h in range(4):
            for i in range(2):
                pe.matmul(k.bank[h][:, i * n:(i + 1) * n], self.w[i][:, h, :], self.conv[:, h, :], start=True, stop=True)
            pe.matmul(k.bank[4 + h // 2][:, (h % 2) * n:(h % 2 + 1) * n], self.w[2][:, h, :], self.xT[:, h, :], start=True, stop=True)
            for t in range(TT):
                last = pe.matmul(k.bank[6 + t][:, h * P:(h + 1) * P], self.xT[:, h, t * P:(t + 1) * P], self.w[2][:, h, :], start=True, stop=True)
        last.then_inc(self.projected, 1)
        pe.wait_ge(self.read_act, 4)
        pe.wait_ge(self.read_dve, 4)
        for i in range(2):
            for h in range(4):
                for j in range(3):
                    rhs = self.qk[:, h, j, :] if j < 2 else self.vT[:, h, :]
                    last = pe.matmul(k.bank[0][0:4, i * n:(i + 1) * n], self.w_if[:, 3 * h + j, 4 * i:4 * i + 4], rhs,
                                     start=h == 0 and j == 0, stop=h == 3 and j == 2)
        last.then_inc(self.gated, 1)
        pe.wait_ge(self.rows_ready, 1)
        for t in range(TT):
            for i, r in enumerate((3, 5)):
                last = pe.transpose(k.bank[1][:, (2 * t + i) * 4:(2 * t + i + 1) * 4], self.rows[0:4, r, t * P:(t + 1) * P], k.c("ident", 0, 4)[0:4, :])
        last.then_inc(self.cols_turned, 1)
        for h in range(4):
            if h:
                pe.wait_ge(self.weighted, h)
            spread = k.c("rowsel", h * P, (h + 1) * P)[0:4, :]
            pe.matmul(k.bank[2][:, 0:n], spread, self.rows[0:4, 4, :], start=True, stop=True)
            pe.matmul(k.bank[2][:, n:n + P], spread, self.rows[0:4, 4, P:n], start=True, stop=True)
            q, kk = self.qk[:, h, 0, :], self.qk[:, h, 1, :]
            pe.matmul(k.bank[3][:, 0:n], kk[:, 0:P], q, start=True, stop=True)
            pe.matmul(k.bank[3][:, n:n + P], kk[:, P:n], q[:, P:n], start=True, stop=True).then_inc(self.scored, 1)
            pe.wait_ge(self.weighted, h + 1)
            if h:
                pe.wait_ge(self.mean, h)
            w = self.weights
            for t in range(TT):
                bank = k.bank[4 + t][:, 0:129]
                pe.matmul(bank, w[:, t * P:(t + 1) * P], self.v[:, 0, h, :], start=True, stop=t == 0)
                if t:
                    last = pe.matmul(bank, w[:, 2 * P:3 * P], self.v[:, 1, h, :], start=False, stop=True)
            last.then_inc(self.summed, 1)

    def scalar(self, act):
        k, n = self.k, TOKENS
        wait_all(act, self.before)
        act.wait_ge(self.convolved, 1)
        act.activation(self.conv, self.conv, ACT.Silu).then_inc(self.silu, 1)
        act.wait_ge(self.projected, 1)
        for h in range(4):
            act.copy(self.qk[:, h, :, :].rearrange("p i n -> p (i n)"), k.bank[h][:, :]).then_inc(self.read_act, 1)
        act.preload_act_table_set("natural_log_exp_and_others")
        act.wait_ge(self.gate_in, 1)
        r = self.rows[0:4]
        k.act_link(act, act.activation(r[:, 6, :], r[:, 1, :], ACT.Abs))
        k.act_link(act, act.activation(r[:, 6, :], r[:, 6, :], ACT.Exp, scale=-1.0))
        act.activation(r[:, 6, :], r[:, 6, :], ACT.Ln, bias=1.0).then_inc(self.gate_log, 1)
        act.wait_ge(self.cols_read, 1)
        act.activation(self.cols[:, :, 1, :], self.cols[:, :, 1, :], ACT.Exp).then_inc(self.expm, 1)
        for h in range(4):
            act.wait_ge(self.masked, h + 1)
            act.activation(self.e[:, 0:n], k.bank[2][:, 0:n], ACT.Exp, scale=-1.0, bias=self.cols[:, 0, 0, h:h + 1])
            act.activation(self.e[:, n:n + P], k.bank[2][:, n:n + P], ACT.Exp, scale=-1.0, bias=self.cols[:, 1, 0, h:h + 1]).then_inc(self.exped, 1)

    def vector(self, dve):
        k, n = self.k, TOKENS
        link = lambda ins: k.dve_link(dve, ins)
        wait_all(dve, self.before)
        for c in range(4):
            last = dve.tensor_scalar(self.conv[:, c, :], self.xT[:, c, :], k.col("conv_w_2_3", c), k.col("conv_b_2", c), ALU.mult, ALU.add)
        link(last)
        for tap, back in ((2, 1), (1, 2), (0, 3)):
            for c in range(4):
                acc = self.conv[:, c, back:n]
                last = dve.scalar_tensor_tensor(acc, self.xT[:, c, 0:n - back], k.col(f"conv_w_2_{tap}", c), acc, ALU.mult, ALU.add)
            if tap:
                link(last)
        last.then_inc(self.convolved, 1)
        dve.wait_ge(self.projected, 1)
        for i in range(2):
            dve.tensor_copy(self.vT[:, 2 * i:2 * i + 2, :].rearrange("p h n -> p (h n)"), k.bank[4 + i][:, :]).then_inc(self.read_dve, 1)
        for t in range(TT):
            dve.tensor_copy(self.v[:, t, :, 0:P], k.bank[6 + t].rearrange("p (h n) -> p h n", h=4)).then_inc(self.read_dve, 1)
        link(dve.memset(self.v[:, :, :, P:P + 1], 1.0))
        r = self.rows[0:4]
        dve.wait_ge(self.gated, 1)
        dve.tensor_scalar(r[:, 0, :], k.bank[0][0:4, 0:n], self.b_if[0:4, 0:1], None, ALU.add)
        dve.tensor_scalar(r[:, 1, :], k.bank[0][0:4, n:2 * n], self.b_if[0:4, 1:2], None, ALU.add).then_inc(self.gate_in, 1)
        dve.wait_ge(self.gate_log, 1)
        link(dve.scalar_tensor_tensor(r[:, 6, :], r[:, 1, :], 0.0, r[:, 6, :], ALU.min, ALU.subtract))
        ones = k.c("ones")[0:4, :]
        link(dve.tensor_tensor_scan(r[:, 2, :], ones, r[:, 6, :], 0.0, ALU.mult, ALU.add))
        link(dve.tensor_tensor(r[:, 3, :], r[:, 0, :], r[:, 2, :], ALU.subtract))
        link(dve.tensor_tensor_scan(r[:, 4, :], ones, r[:, 3, :], 0.0, ALU.mult, ALU.max))
        dve.scalar_tensor_tensor(r[:, 5, :], r[:, 2, :], -1.0, r[:, 4, :], ALU.mult, ALU.subtract).then_inc(self.rows_ready, 1)
        dve.wait_ge(self.cols_turned, 1)
        dve.tensor_copy(self.cols.rearrange("p t i h -> p (t i h)"), k.bank[1][:, 0:16]).then_inc(self.cols_read, 1)
        diagonal = StickBreaking._diagonal
        mask = k.c("causalT").unsqueeze(1).broadcast_to([P, 2, P])
        for h in range(4):
            dve.wait_ge(self.scored, h + 1)
            d = diagonal(k.bank[2][:, 0:384])
            dve.tensor_tensor(d, d, mask, ALU.subtract).then_inc(self.masked, 1)
            dve.wait_ge(self.exped, h + 1)
            if h:
                dve.wait_ge(self.summed, h)
            dve.scalar_tensor_tensor(self.weights, k.bank[3][:, 0:384], P ** -0.5, self.e, ALU.mult, ALU.mult).then_inc(self.weighted, 1)
            dve.wait_ge(self.summed, h + 1)
            dve.wait_ge(self.expm, 1)
            for t in range(TT):
                st = self.stat[:, 0, 2 * t:2 * t + 1]
                den = k.bank[4 + t][:, P:P + 1]
                link(dve.tensor_scalar(st, den, -1.0, self.cols[:, t, 1, h:h + 1], ALU.mult, ALU.max))
                link(dve.tensor_tensor(st, den, st, ALU.max))
                link(dve.reciprocal(st, st))
                last = dve.tensor_scalar(k.y[:, t, 512 + h * P:512 + (h + 1) * P], k.bank[4 + t][:, 0:P], st, None, ALU.mult)
            last.then_inc(self.mean, 1)
        dve.wait_ge(self.mean, 4)
        view = [k.y[:, t, 512:1024].rearrange("p (h n) -> p h n", h=4) for t in range(TT)]
        wide = lambda i, t: self.stat[:, i, 4 * t:4 * t + 4].unsqueeze(2).broadcast_to([P, 4, P])
        for t in range(TT):
            last = dve.tensor_reduce(self.stat[:, 0, 4 * t:4 * t + 4], view[t], AX.X, ALU.add)
        link(last)
        link(dve.tensor_scalar(self.stat[:, 0, :], self.stat[:, 0, :], 1.0 / P, None, ALU.mult))
        for t in range(TT):
            last = dve.tensor_tensor(view[t], view[t], wide(0, t), ALU.subtract)
        link(last)
        sq = self.qk.rearrange("p h i n -> p (h i n)")[:, 0:1024].rearrange("p (t h n) -> p t h n", t=TT, h=4)
        for t in range(TT):
            last = dve.tensor_tensor(sq[:, t], view[t], view[t], ALU.mult)
        link(last)
        for t in range(TT):
            last = dve.tensor_reduce(self.stat[:, 1, 4 * t:4 * t + 4], sq[:, t], AX.X, ALU.add)
        last.then_inc(self.squares, 1)
        dve.wait_ge(self.rstd, 1)
        for t in range(TT):
            last = dve.tensor_tensor(view[t], view[t], wide(3, t), ALU.mult)
        last.then_inc(self.normed, 1)


class MlstmOut(Stage):

    def __init__(self, core, before, hT, conv, zT):
        super().__init__(core, before)
        self.aT, self.hT, self.conv, self.zT = hT[:, 0:4, :], hT[:, 4:8, :], conv, zT
        self.s0 = core.silu_ready.plan(1)
        self.d0 = core.product_done.plan(1)
        self.done = self.before + [(core.product_done.sem, self.d0 + 1)]

    def scalar(self, act):
        wait_all(act, self.before)
        act.activation(self.zT, self.zT, ACT.Silu).then_inc(self.k.silu_ready.sem, 1)

    def vector(self, dve):
        k = self.k
        wait_all(dve, self.before)
        for c in range(4):
            last = dve.scalar_tensor_tensor(self.hT[:, c, :], self.conv[:, c, :], k.col("mlstm_skip_2", c), self.hT[:, c, :], ALU.mult, ALU.add)
        k.dve_link(dve, last)
        feat_from(k, dve, self.aT, 0, 4)
        dve.wait_ge(k.silu_ready.sem, self.s0 + 1)
        k.dve_link(dve, dve.tensor_tensor(self.hT, self.hT, self.zT, ALU.mult))
        feat_from(k, dve, self.hT, 4, 8).then_inc(k.product_done.sem, 1)


def hybrid(core, before, mod):
    k = core
    proj = Linear(k, before, "w_in_2", "store", dst=k.proj)
    early = Presplit(k, proj)
    T = heads_view(k, 0, 16)
    cols = [0, 128, 256, 384, 512, 640, 768, 896] + [1536 + i * P for i in range(8)]
    turn = Turn(k, proj, lambda t, c: k.proj[:, t, cols[c]:cols[c] + P], T, 16)
    rows = lambda h: slice((h % 2) * HEAD, (h % 2 + 1) * HEAD)

    def job(h):
        return Job(lambda t: T[rows(h), h // 2, t * P:(t + 1) * P], lambda lo, hi: T[rows(h), 4 + h // 2, lo:hi],
                   lambda t: k.proj[:, t, 1024 + h * HEAD:1024 + (h + 1) * HEAD])
    att = Attention(k, turn, [[(s, job(4 * g + s)) for s in range(4)] for g in range(2)], "causal", 4096, k.y)
    lstm = Mlstm(k, att, T[:, 8:12, :], 4096)
    half = lambda g: k.y[:, g, 0:512]
    rs = Rstd(k, lstm, half, TT, 512, out=half)
    hT = heads_view(k, 0, KC)
    gain = lambda c: k.col("attn_norm_2", c) if c < 4 else k.col("mlstm_norm_2", c - 4)
    back = Turn(k, rs, lambda t, c: k.y[:, t, c * P:(c + 1) * P], hT, KC, scale=gain)
    out = MlstmOut(k, back, hT, lstm.conv, T[:, 12:16, :])
    gate = GateRow(k, out, mod, 1)
    return [proj, early, turn, att, lstm, rs, back, out, gate, Linear(k, gate, "w_out_2", k.row)]


class Gla(Stage):

    def __init__(self, core, before, qT, kT, at):
        super().__init__(core, before)
        k = core
        self.qT, self.kT = qT, kT
        a = k.arena

        def take(size):
            nonlocal at
            at += size
            return a[:, at - size:at]

        n = TOKENS
        self.w_up = take(512)
        self.low = take(n)
        self.gate = take(4 * n).rearrange("p (h n) -> p h n", h=4)
        self.cum = take(4 * n).rearrange("p (h n) -> p h n", h=4)
        self.f = take(4 * n)
        self.qf = [take(4 * n).rearrange("p (h n) -> p h n", h=4) for _ in range(2)]
        self.kf = [take(4 * n).rearrange("p (h n) -> p h n", h=4) for _ in range(2)]
        self.part = take(1024)
        self.s = take(1024).rearrange("p (b n) -> p b n", b=8)
        self.cross = take(512).rearrange("p (b n) -> p b n", b=4)
        self.levels = LEVELS + [TOKENS]
        assert at <= ARENA
        nl = len(self.levels)
        self.w_landed = k.sig("g_w_landed").sem
        self.low_turned = k.sig("g_low_turned").sem
        self.low_read = k.sig("g_low_read").sem
        self.gated = k.sig("g_gated").sem
        self.gate_in = k.sig("g_gate_in").sem
        self.gate_log = k.sig("g_gate_log").sem
        self.cum_ready = k.sig("g_cum_ready").sem
        self.apart = k.sig("g_apart").sem
        self.factor = k.sig("g_factor").sem
        self.q_ready = k.sig("g_q_ready").sem
        self.k_ready = k.sig("g_k_ready").sem
        self.scored = k.sig("g_scored").sem
        self.parted = k.sig("g_parted").sem
        self.added = k.sig("g_added").sem
        self.valued = k.sig("g_valued").sem
        self.out_read = k.sig("g_out_read").sem
        self.done = [(self.out_read, 4)]

    def gpsimd(self, pool):
        k = self.k
        wait_all(pool, self.before)
        pool.dma_start(self.w_up[0:16, :], k.dram["gla_w_gate_up_3"]).then_inc(self.w_landed, 16)
        for l in range(len(self.levels)):
            pool.wait_ge(self.factor, l + 1)
            if l >= 2:
                pool.wait_ge(self.scored, l)
            pool.tensor_tensor(self.kf[l % 2].rearrange("p h n -> p (h n)"), self.kT.rearrange("p h n -> p (h n)"), self.f, ALU.mult).then_inc(self.k_ready, 1)

    def tensor(self, pe):
        k, n = self.k, TOKENS
        wait_all(pe, self.before)
        for t in range(TT):
            last = pe.transpose(k.bank[0][0:16, t * P:(t + 1) * P], k.proj[:, t, 3072:3088], k.c("ident"))
        last.then_inc(self.low_turned, 1)
        pe.wait_ge(self.low_read, 1)
        pe.wait_ge(self.w_landed, 16)
        for h in range(4):
            last = pe.matmul(k.bank[1 + h // 2][:, (h % 2) * n:(h % 2 + 1) * n], self.w_up[0:16, h * P:(h + 1) * P], self.low[0:16, :], start=True, stop=True)
        last.then_inc(self.gated, 1)

        def tile_products(q, kk):
            for h in range(4):
                for t in range(TT):
                    b = 2 * h + t
                    last = pe.matmul(k.bank[3 + b // 4][:, (b % 4) * P:(b % 4 + 1) * P], kk[:, h, t * P:(t + 1) * P], q[:, h, t * P:(t + 1) * P],
                                     start=True, stop=True)
            last.then_inc(self.scored, 1)

        tile_products(self.qT, self.kT)
        for l, b in enumerate(self.levels):
            pe.wait_ge(self.q_ready, l + 1)
            pe.wait_ge(self.k_ready, l + 1)
            pe.wait_ge(self.parted, l + 1)
            q, kk = self.qf[l % 2], self.kf[l % 2]
            if b < n:
                tile_products(q, kk)
            else:
                for h in range(4):
                    last = pe.matmul(k.bank[3][:, h * P:(h + 1) * P], kk[:, h, 0:P], q[:, h, P:n], start=True, stop=True)
                last.then_inc(self.scored, 1)
        pe.wait_ge(self.added, len(LEVELS) + 2)
        for h in range(4):
            v = lambda t: k.proj[:, t, D + h * 256:D + (h + 1) * 256]
            if h >= 2:
                pe.wait_ge(self.out_read, h - 1)
            bank = k.bank[h % 2]
            pe.matmul(bank[:, 0:256], self.s[:, 2 * h, :], v(0), start=True, stop=True)
            pe.matmul(bank[:, 256:512], self.cross[:, h, :], v(0), start=True, stop=False)
            pe.matmul(bank[:, 256:512], self.s[:, 2 * h + 1, :], v(1), start=False, stop=True).then_inc(self.valued, 1)

    def scalar(self, act):
        k = self.k
        wait_all(act, self.before)
        act.preload_act_table_set("natural_log_exp_and_others")
        act.wait_ge(self.gate_in, 1)
        e = self.f
        g = self.gate.rearrange("p h n -> p (h n)")
        k.act_link(act, act.activation(e, g, ACT.Abs))
        k.act_link(act, act.activation(e, e, ACT.Exp, scale=-1.0))
        act.activation(e, e, ACT.Ln, bias=1.0).then_inc(self.gate_log, 1)
        for l in range(len(self.levels)):
            act.wait_ge(self.apart, l + 1)
            k.act_link(act, act.activation(self.f, self.f, ACT.Abs))
            act.activation(self.f, self.f, ACT.Exp, scale=-1.0 / 16.0).then_inc(self.factor, 1)

    def vector(self, dve):
        k, n = self.k, TOKENS
        link = lambda ins: k.dve_link(dve, ins)
        wait_all(dve, self.before)
        dve.wait_ge(self.low_turned, 1)
        dve.tensor_copy(self.low[0:16, :], k.bank[0][0:16, 0:n]).then_inc(self.low_read, 1)
        dve.wait_ge(self.gated, 1)
        for h in range(4):
            last = dve.tensor_scalar(self.gate[:, h, :], k.bank[1 + h // 2][:, (h % 2) * n:(h % 2 + 1) * n], k.col("gla_b_gate_3", h), None, ALU.add)
        last.then_inc(self.gate_in, 1)
        dve.wait_ge(self.gate_log, 1)
        flat = lambda x: x.rearrange("p h n -> p (h n)")
        link(dve.scalar_tensor_tensor(flat(self.gate), flat(self.gate), 0.0, self.f, ALU.min, ALU.subtract))
        for h in range(4):
            last = dve.tensor_tensor_scan(self.cum[:, h, :], k.c("ones"), self.gate[:, h, :], 0.0, ALU.mult, ALU.add)
        link(last)

        def take_apart(mask, l, cross):
            dve.wait_ge(self.scored, l + 1)
            if cross:
                dve.tensor_copy(self.cross.rearrange("p b n -> p (b n)"), k.bank[3][:]).then_inc(self.added, 1)
                return
            part = self.part.rearrange("p (b n) -> p b n", b=8)
            out = self.s if l == 0 else part
            for i in range(2):
                last = dve.tensor_tensor(out[:, 4 * i:4 * i + 4, :], k.bank[3 + i][:, :].rearrange("p (b n) -> p b n", b=4),
                                         k.c(mask).unsqueeze(1).broadcast_to([P, 4, P]), ALU.mult)
            last.then_inc(self.parted, 1)
            dve.wait_ge(self.parted, l + 1)
            if l == 0:
                link(dve.memset(k.small[:, 63:64], 0.0))
                dve.memset(k.small[:, 62:63], 0.0).then_inc(self.added, 1)
            else:
                dve.tensor_tensor(flat(self.s), flat(self.s), self.part, ALU.add).then_inc(self.added, 1)
                dve.wait_ge(self.added, l + 1)

        for l, b in enumerate(self.levels):
            if l:
                dve.wait_ge(self.q_ready, l)
                dve.wait_ge(self.k_ready, l)
            c3 = flat(self.cum).rearrange("p (m b) -> p m b", b=b)
            f3 = self.f.rearrange("p (m b) -> p m b", b=b)
            dve.tensor_tensor(f3, c3, c3[:, :, b // 2 - 1:b // 2].broadcast_to([P, 4 * n // b, b]), ALU.subtract).then_inc(self.apart, 1)
            take_apart("ident" if l == 0 else f"level{self.levels[l - 1]}", l, False)
            dve.wait_ge(self.factor, l + 1)
            dve.tensor_tensor(flat(self.qf[l % 2]), flat(self.qT), self.f, ALU.mult).then_inc(self.q_ready, 1)
        take_apart(None, len(self.levels), True)
        for h in range(4):
            dve.wait_ge(self.valued, h + 1)
            dve.tensor_copy(k.y[:, :, h * 256:(h + 1) * 256], k.bank_tiles(h % 2)).then_inc(self.out_read, 1)


def gla(core, before):
    k = core
    proj = Linear(k, before, "gla_w_in_3", "store", dst=k.proj)
    early = Presplit(k, proj)
    T = heads_view(k, 0, 8)
    turn = Turn(k, proj, lambda t, c: k.proj[:, t, c * P:(c + 1) * P], T, 8, scale=lambda c: P ** -0.5 if c < 4 else 1.0)
    att = Gla(k, turn, T[:, 0:4, :], T[:, 4:8, :], 8 * TOKENS)
    part = lambda g: k.y[:, g // 4, (g % 4) * 256:(g % 4 + 1) * 256]
    rs = Rstd(k, att, part, 8, 256, out=part)
    prod = Product(k, rs, lambda t: k.y[:, t, :], lambda t: k.proj[:, t, 2 * D:3 * D], lambda t: k.y[:, t, :], silu=True)
    back = FeatTurn(k, prod, lambda t, c: k.y[:, t, c * P:(c + 1) * P], scale=lambda c: k.col("gla_head_norm_3", c))
    return [proj, early, turn, att, rs, prod, back, Linear(k, back, "gla_w_o_3", "y")]


def network(core):
    k = core
    mod = Modulation(k)
    plan = [Load(k)]

    def feed(norm, w_in, w_down, how, silu=True, branch=None, part=None):
        if branch is None:
            plan.extend(pre_norm(k, plan[-1], norm))
        else:
            plan.extend(pre_norm(k, plan[-1], None, mod.scale(branch), mod.shift(branch)))
        if part is not None:
            plan.append(ModPart(k, plan[-1], mod, part))
        if branch is not None:
            plan.append(GateRow(k, plan[-1], mod, branch))
        plan.append(FeedForward(k, plan[-1], w_in, w_down, silu, how))
        if part is not None:
            plan.append(ModSpread(k, plan[-1], mod, part, ("ffn1_norm_2", "mix_norm_2", "ffn2_norm_2")[part]))

    for l, mixer in enumerate((nsa, swa)):
        feed(f"ffn1_norm{l}", f"ffn1_in{l}", f"ffn1_down{l}", "half", part=2 * l)
        plan.extend(pre_norm(k, plan[-1], f"mix_norm{l}"))
        plan.extend(mixer(k, plan[-1]))
        feed(f"ffn2_norm{l}", f"ffn2_in{l}", f"ffn2_down{l}", "half", part=1 if l == 0 else None)
    plan.extend(row_norm(k, plan[-1], "final_norm"))
    feed(None, "ffn1_in_2", "ffn1_down_2", k.row, branch=0)
    plan.extend(pre_norm(k, plan[-1], None, mod.scale(1), mod.shift(1)))
    plan.extend(hybrid(k, plan[-1], mod))
    feed(None, "ffn2_in_2", "ffn2_down_2", k.row, branch=2)
    plan.extend(row_norm(k, plan[-1], "final_norm_2"))
    mixers = (lambda b: stick_breaking(k, b, "sb_w_qkv_3_0", "sb_w_o_3_0"), lambda b: short_conv(k, b), lambda b: gla(k, b),
              lambda b: stick_breaking(k, b, "sb_w_qkv_3_1", "sb_w_o_3_1"))
    for i in range(4):
        plan.extend(pre_norm(k, plan[-1], f"norm_gains_3_{i}0"))
        plan.extend(mixers[i](plan[-1]))
        plan.extend(post_norm(k, plan[-1], f"norm_gains_3_{i}1"))
        feed(f"norm_gains_3_{i}2", f"ffn_in_3_{i}", f"ffn_down_3_{i}", "y", silu=False)
        plan.extend(post_norm(k, plan[-1], f"norm_gains_3_{i}3"))
    plan.append(Store(k, plan[-1]))
    return plan


def build(nc, dram):
    with ExitStack() as ctx:
        core = Core(nc, ctx, dram)
        plan = network(core)
        block = ctx.enter_context(nc.Block())

        @block.sync
        def _(sp):
            for stage in plan:
                stage.sync(sp)

        @block.tensor
        def _(pe):
            for stage in plan:
                stage.tensor(pe)

        @block.scalar
        def _(act):
            for stage in plan:
                stage.scalar(act)

        @block.vector
        def _(dve):
            for stage in plan:
                stage.vector(dve)

        @block.gpsimd
        def _(pool):
            for stage in plan:
                stage.gpsimd(pool)


def glu_units(w):
    n = w.shape[1] // (2 * P)
    a = w.reshape(KC, P, 2, n, P).transpose(3, 1, 2, 0, 4)
    return np.ascontiguousarray(a).reshape(n, P, UNIT)


def up_units(w):
    n = w.shape[1] // (2 * P)
    a = w.reshape(KC, P, n, 2, P).transpose(2, 1, 3, 0, 4)
    return np.ascontiguousarray(a).reshape(n, P, UNIT)


def down_units(w, chunks):
    n = w.shape[0] // (P * chunks)
    return np.ascontiguousarray(w.reshape(n, chunks, P, D).transpose(0, 2, 1, 3)).reshape(n, P, chunks * D)


def arrays_of(a):
    out = {"x": a["x"].reshape(TOKENS, D)}
    t = constant_table()
    out["const"] = np.concatenate([t[n] for n in CONST_COLS], 1)
    vec = {}
    for l in range(2):
        for n in ("ffn1_norm", "mix_norm", "ffn2_norm"):
            vec[f"{n}{l}"] = a[n][l]
    for n in ("ffn1_norm_2", "mix_norm_2", "ffn2_norm_2", "conv_b_2", "mlstm_norm_2", "mlstm_skip_2", "attn_norm_2"):
        vec[n] = a[n][0]
    for i in range(4):
        vec[f"conv_w_2_{i}"] = a["conv_w_2"][0, i]
        for j in range(4):
            vec[f"norm_gains_3_{i}{j}"] = a["norm_gains_3"][i, j]
    for i in range(3):
        vec[f"conv_w_3_{i}"] = a["conv_w_3"][0, i]
    vec["gla_head_norm_3"] = a["gla_head_norm_3"][0].reshape(-1)
    vec["gla_b_gate_3"] = a["gla_b_gate_3"][0]
    vec["c_2"] = a["c_2"][0]
    vec["ck_pe"], vec["cv_pe"] = a["nsa_ck_pe"][0].reshape(-1), a["nsa_cv_pe"][0].reshape(-1)
    vec["final_norm"], vec["final_norm_2"] = a["final_norm"], a["final_norm_2"]
    out["cols"] = np.concatenate([vec[n].reshape(-1, P).T for n, _ in COLUMN_VECTORS], 1)
    out["rows"] = np.stack([vec[n] for n in ROW_VECTORS])
    for l in range(2):
        for f in (1, 2):
            out[f"ffn{f}_in{l}"] = glu_units(a[f"ffn{f}_w_gu"][l])
            out[f"ffn{f}_down{l}"] = down_units(a[f"ffn{f}_w_down"][l], 1)
    for f in (1, 2):
        out[f"ffn{f}_in_2"] = glu_units(np.concatenate([a[f"ffn{f}_w_gate_2"][0], a[f"ffn{f}_w_up_2"][0]], 1))
        out[f"ffn{f}_down_2"] = down_units(a[f"ffn{f}_w_down_2"][0], 1)
    for i in range(4):
        out[f"ffn_in_3_{i}"] = up_units(a["ffn_w_up_3"][i])
        out[f"ffn_down_3_{i}"] = down_units(a["ffn_w_down_3"][i], 2)
    for n, m in (("nsa_w_in", "nsa_w_in"), ("nsa_w_out", "nsa_w_out"), ("swa_w_in", "swa_w_in"), ("swa_w_out", "swa_w_out"),
                 ("w_in_2", "w_in_2"), ("w_out_2", "w_out_2"), ("w_ada_2", "w_ada_2"), ("b_ada_2", "b_ada_2"),
                 ("conv_w_in_3", "conv_w_in_3"), ("conv_w_out_3", "conv_w_out_3"), ("gla_w_in_3", "gla_w_in_3"),
                 ("gla_w_gate_up_3", "gla_w_gate_up_3"), ("gla_w_o_3", "gla_w_o_3"), ("w_q_m_2", "w_q_m_2"),
                 ("w_k_m_2", "w_k_m_2"), ("w_v_m_2", "w_v_m_2"), ("w_if_2", "w_if_2"),
                 ("nsa_ck_w1", "nsa_ck_w1"), ("nsa_cv_w1", "nsa_cv_w1"), ("nsa_ck_w2", "nsa_ck_w2"),
                 ("nsa_cv_w2", "nsa_cv_w2"), ("swa_sinks", "swa_sinks")):
        out[n] = a[m][0] if a[m].ndim > 2 else a[m]
    for i in range(2):
        out[f"sb_w_qkv_3_{i}"], out[f"sb_w_o_3_{i}"] = a["sb_w_qkv_3"][i], a["sb_w_o_3"][i]
    out["b_if_2"] = a["b_if_2"].reshape(2, 4).T
    return out


def kernel(**inputs):
    import concourse.bacc as bacc
    from concourse.bass_utils import run_bass_kernel_spmd

    a = {n: np.asarray(v) for n, v in inputs.items()}
    arrays = {f"in_{n}": np.ascontiguousarray(v) for n, v in arrays_of(a).items()}
    nc = bacc.Bacc("TRN2", target_bir_lowering=False, num_devices=1)
    dram = {n[3:]: nc.dram_tensor(n, v.shape, F32, kind="ExternalInput").ap() for n, v in arrays.items()}
    dram["out"] = nc.dram_tensor("out", (TOKENS, D), F32, kind="ExternalOutput").ap()
    build(nc, dram)
    result = run_bass_kernel_spmd(nc, [arrays], core_ids=[0])
    return result.results[0]["out"].reshape(1, TOKENS, D)
```
